# Optimizing a Trainium2 kernel written in Bass

```python
import math
import jax, jax.numpy as jnp
from jax import lax
import numpy as np

D_MODEL = 1024
BATCH = 1
SEQ = 256
DEPTH = 2

CONV_CH = D_MODEL // 4
CONV_WIDTH = 31
MOBA_HEADS = 4
MOBA_HEAD_DIM = D_MODEL // 16
MOBA_WIDTH = MOBA_HEADS * MOBA_HEAD_DIM
MOBA_BLOCK = 256
MOBA_TOPK = 3
MOBA_Q_CHUNK = 64
GLA_HEADS = 4
GLA_WIDTH = D_MODEL // 2
GLA_DV = GLA_WIDTH // GLA_HEADS
GLA_DK = GLA_DV // 2
GLA_GATE_RANK = 16
GLA_TAU = 16.0
GLA_CHUNK = 32
MIX_WIDTH = CONV_CH + MOBA_WIDTH + GLA_WIDTH
D_FF = 2816
FFN_CONV_WIDTH = 3
NORM_EPS = 1e-6
NEG_INF = -1e30

COL_A = 2 * CONV_CH
COL_B = 3 * MOBA_WIDTH
COL_C_Q = GLA_HEADS * GLA_DK
COL_C_K = GLA_HEADS * GLA_DK
COL_C_V = GLA_WIDTH
COL_C_G = GLA_GATE_RANK
COL_C_R = GLA_WIDTH
COL_C = COL_C_Q + COL_C_K + COL_C_V + COL_C_G + COL_C_R
IN_COLS = COL_A + COL_B + COL_C


def rms_norm(x, g, eps=NORM_EPS):
    xf = x.astype(jnp.float32)
    y = xf * lax.rsqrt(jnp.mean(xf * xf, axis=-1, keepdims=True) + eps)
    return (y * g.astype(jnp.float32)).astype(x.dtype)

def head_rms_norm(x, g, n_heads):
    B, S, W = x.shape
    xf = x.astype(jnp.float32).reshape(B, S, n_heads, W // n_heads)
    y = xf * lax.rsqrt(jnp.mean(xf * xf, axis=-1, keepdims=True) + NORM_EPS)
    return (y.reshape(B, S, W) * g.astype(jnp.float32)).astype(x.dtype)

def layer_norm(x, g, b, eps=1e-5):
    xf = x.astype(jnp.float32)
    mu = jnp.mean(xf, axis=-1, keepdims=True)
    var = jnp.mean(jnp.square(xf - mu), axis=-1, keepdims=True)
    y = (xf - mu) * lax.rsqrt(var + eps)
    return (y * g.astype(jnp.float32) + b.astype(jnp.float32)).astype(x.dtype)

def causal_depthwise_conv(x, w, b):
    W = w.shape[0]
    y = lax.conv_general_dilated(
        x, w[:, None, :].astype(x.dtype), window_strides=(1,), padding=[(W - 1, 0)],
        dimension_numbers=("NWC", "WIO", "NWC"), feature_group_count=x.shape[-1])
    return y + b.astype(x.dtype)

def conformer_conv(a_val, a_gate, conv_w, conv_b, ln_g, ln_b):
    h = a_val * jax.nn.sigmoid(a_gate)
    h = causal_depthwise_conv(h, conv_w, conv_b)
    h = layer_norm(h, ln_g, ln_b)
    return jax.nn.silu(h)

def moba_attention(q, k, v):
    B, S, H, dh = q.shape
    s_pad = ((S + MOBA_BLOCK - 1) // MOBA_BLOCK) * MOBA_BLOCK
    pad = [(0, 0), (0, s_pad - S), (0, 0), (0, 0)]
    qp = jnp.pad(q, pad).transpose(0, 2, 1, 3)
    kp = jnp.pad(k, pad).transpose(0, 2, 1, 3)
    vp = jnp.pad(v, pad).transpose(0, 2, 1, 3)
    nb = s_pad // MOBA_BLOCK
    topk = min(MOBA_TOPK, nb)
    kb = kp.reshape(B, H, nb, MOBA_BLOCK, dh)
    vb = vp.reshape(B, H, nb, MOBA_BLOCK, dh)
    k_mean = jnp.mean(kb.astype(jnp.float32), axis=3)
    nq = s_pad // MOBA_Q_CHUNK
    q_chunks = qp.reshape(B, H, nq, MOBA_Q_CHUNK, dh).transpose(2, 0, 1, 3, 4)
    scale = 1.0 / math.sqrt(dh)
    chunks_per_block = MOBA_BLOCK // MOBA_Q_CHUNK
    gather_blocks = jax.vmap(jax.vmap(lambda t, i: t[i]))

    def one_chunk(args):
        c, qc = args
        own = c // chunks_per_block
        q_pos = c * MOBA_Q_CHUNK + jnp.arange(MOBA_Q_CHUNK)
        gate = jnp.einsum("bhqd,bhnd->bhqn", qc.astype(jnp.float32), k_mean)
        gate = jnp.where(jnp.arange(nb) < own, gate, NEG_INF)
        _, idx = lax.top_k(gate, topk)
        valid = idx < own
        ks = gather_blocks(kb, idx)
        vs = gather_blocks(vb, idx)
        l_sel = jnp.einsum("bhqd,bhqtkd->bhqtk", qc, ks).astype(jnp.float32) * scale
        l_sel = jnp.where(valid[..., None], l_sel, NEG_INF).reshape(B, H, MOBA_Q_CHUNK, topk * MOBA_BLOCK)
        k_own = lax.dynamic_index_in_dim(kb, own, axis=2, keepdims=False)
        v_own = lax.dynamic_index_in_dim(vb, own, axis=2, keepdims=False)
        k_pos = own * MOBA_BLOCK + jnp.arange(MOBA_BLOCK)
        l_own = jnp.einsum("bhqd,bhkd->bhqk", qc, k_own).astype(jnp.float32) * scale
        l_own = jnp.where(k_pos[None, :] <= q_pos[:, None], l_own, NEG_INF)
        p = jax.nn.softmax(jnp.concatenate([l_sel, l_own], axis=-1), axis=-1)
        p_sel = p[..., : topk * MOBA_BLOCK].reshape(B, H, MOBA_Q_CHUNK, topk, MOBA_BLOCK).astype(vs.dtype)
        p_own = p[..., topk * MOBA_BLOCK:].astype(v_own.dtype)
        return (jnp.einsum("bhqtk,bhqtkd->bhqd", p_sel, vs)
                + jnp.einsum("bhqk,bhkd->bhqd", p_own, v_own))

    out = lax.map(one_chunk, (jnp.arange(nq), q_chunks))
    out = out.transpose(1, 0, 3, 2, 4).reshape(B, s_pad, H, dh)
    return out[:, :S].astype(q.dtype)

def gla_chunked(q, k, v, log_a):
    B, S, H, DK = q.shape
    DV = v.shape[-1]
    C = GLA_CHUNK
    nc = S // C

    def to_chunks(t):
        return t.astype(jnp.float32).reshape(B, nc, C, H, t.shape[-1]).transpose(0, 3, 1, 2, 4)

    qc, kc, vc, gc = to_chunks(q), to_chunks(k), to_chunks(v), to_chunks(log_a)
    G = jnp.cumsum(gc, axis=3)
    gamma = G[:, :, :, -1:, :]
    qg = qc * jnp.exp(G)
    kg = kc * jnp.exp(-G)
    kd = kc * jnp.exp(gamma - G)
    tril = jnp.tril(jnp.ones((C, C), dtype=bool))
    attn = jnp.where(tril, jnp.einsum("bhnid,bhnjd->bhnij", qg, kg), 0.0)
    o_intra = jnp.einsum("bhnij,bhnje->bhnie", attn, vc)
    d_state = jnp.einsum("bhnjd,bhnje->bhnde", kd, vc)
    decay = jnp.exp(gamma[:, :, :, 0, :])

    def step(state, inp):
        d, ds = inp
        return d[..., None] * state + ds, state

    _, s_prev = lax.scan(step, jnp.zeros((B, H, DK, DV), jnp.float32),
                         (jnp.moveaxis(decay, 2, 0), jnp.moveaxis(d_state, 2, 0)))
    s_prev = jnp.moveaxis(s_prev, 0, 2)
    o = o_intra + jnp.einsum("bhnid,bhnde->bhnie", qg, s_prev)
    return o.transpose(0, 2, 3, 1, 4).reshape(B, S, H, DV).astype(v.dtype)

def first_inputs(seed: int = 0) -> dict:
    key = jax.random.key(seed)
    ks = jax.random.split(key, 20)
    f32 = jnp.float32
    n = lambda k, shape, s: jax.random.normal(k, shape, f32) * s
    return {
        "x": n(ks[0], (BATCH, SEQ, D_MODEL), 1.0),
        "norm_mix_g": 1.0 + n(ks[1], (DEPTH, D_MODEL), 0.05),
        "w_in": n(ks[2], (DEPTH, D_MODEL, IN_COLS), D_MODEL ** -0.5),
        "conv_w": n(ks[3], (DEPTH, CONV_WIDTH, CONV_CH), CONV_WIDTH ** -0.5),
        "conv_b": n(ks[4], (DEPTH, CONV_CH), 0.02),
        "conv_ln_g": 1.0 + n(ks[5], (DEPTH, CONV_CH), 0.05),
        "conv_ln_b": n(ks[6], (DEPTH, CONV_CH), 0.02),
        "moba_out_g": 1.0 + n(ks[7], (DEPTH, MOBA_WIDTH), 0.05),
        "gla_gate_w": n(ks[8], (DEPTH, GLA_GATE_RANK, GLA_HEADS * GLA_DK), GLA_GATE_RANK ** -0.5),
        "gla_gate_b": n(ks[9], (DEPTH, GLA_HEADS * GLA_DK), 0.1),
        "gla_out_g": 1.0 + n(ks[10], (DEPTH, GLA_WIDTH), 0.05),
        "w_out": n(ks[11], (DEPTH, MIX_WIDTH, D_MODEL), MIX_WIDTH ** -0.5),
        "norm_ffn_g": 1.0 + n(ks[12], (DEPTH, D_MODEL), 0.05),
        "ffn_w_up": n(ks[13], (DEPTH, D_MODEL, 2 * D_FF), D_MODEL ** -0.5),
        "ffn_conv_w": n(ks[14], (DEPTH, FFN_CONV_WIDTH, 2 * D_FF), FFN_CONV_WIDTH ** -0.5),
        "ffn_conv_b": n(ks[15], (DEPTH, 2 * D_FF), 0.02),
        "ffn_w_down": n(ks[16], (DEPTH, D_FF, D_MODEL), D_FF ** -0.5),
        "final_g": 1.0 + n(ks[17], (D_MODEL,), 0.05),
    }

def first_block(x, norm_mix_g, w_in, conv_w, conv_b, conv_ln_g, conv_ln_b, moba_out_g,
              gla_gate_w, gla_gate_b, gla_out_g, w_out, norm_ffn_g, ffn_w_up, ffn_conv_w,
              ffn_conv_b, ffn_w_down, final_g):
    B, S, _ = x.shape
    o1 = COL_A
    o2 = o1 + COL_B
    o3 = o2 + COL_C_Q
    o4 = o3 + COL_C_K
    o5 = o4 + COL_C_V
    o6 = o5 + COL_C_G
    for l in range(DEPTH):
        h = rms_norm(x, norm_mix_g[l])
        p = h @ w_in[l].astype(h.dtype)
        y_a = conformer_conv(p[..., :CONV_CH], p[..., CONV_CH:o1],
                             conv_w[l], conv_b[l], conv_ln_g[l], conv_ln_b[l])
        qkv = p[..., o1:o2].reshape(B, S, 3, MOBA_HEADS, MOBA_HEAD_DIM)
        y_b = moba_attention(qkv[:, :, 0], qkv[:, :, 1], qkv[:, :, 2]).reshape(B, S, MOBA_WIDTH)
        y_b = head_rms_norm(y_b, moba_out_g[l], MOBA_HEADS)
        q_c = p[..., o2:o3].reshape(B, S, GLA_HEADS, GLA_DK) * (GLA_DK ** -0.5)
        k_c = p[..., o3:o4].reshape(B, S, GLA_HEADS, GLA_DK)
        v_c = p[..., o4:o5].reshape(B, S, GLA_HEADS, GLA_DV)
        gate_logit = (p[..., o5:o6] @ gla_gate_w[l].astype(p.dtype)).astype(jnp.float32) \
            + gla_gate_b[l].astype(jnp.float32)
        log_a = (jax.nn.log_sigmoid(gate_logit) / GLA_TAU).reshape(B, S, GLA_HEADS, GLA_DK)
        y_c = gla_chunked(q_c, k_c, v_c, log_a).reshape(B, S, GLA_WIDTH)
        y_c = head_rms_norm(y_c, gla_out_g[l], GLA_HEADS) * jax.nn.silu(p[..., o6:])
        y = jnp.concatenate([y_a, y_b, y_c], axis=-1) @ w_out[l].astype(x.dtype)
        x = x + y
        h = rms_norm(x, norm_ffn_g[l])
        u = causal_depthwise_conv(h @ ffn_w_up[l].astype(h.dtype), ffn_conv_w[l], ffn_conv_b[l])
        x = x + (jax.nn.silu(u[..., :D_FF]) * u[..., D_FF:]) @ ffn_w_down[l].astype(x.dtype)
    return rms_norm(x, final_g)


CTX_LEN = 256
GRID_W = 64
HEAD_DIM = 64
N_HEADS = D_MODEL // HEAD_DIM
NA_HEADS = N_HEADS // 2
WA_HEADS = N_HEADS - NA_HEADS
WA_KV_HEADS = max(1, WA_HEADS // 4)
NA_KH = 8
NA_KW = 16
WA_WINDOW = 128
WA_BLOCK = 128
D_FF_2 = ((8 * D_MODEL // 3 + 127) // 128) * 128
ROPE_BASE = 10000.0
N_MOD = 9
MACARON_W = 0.5
NEG_INF_2 = -1e30
NA_W = NA_HEADS * HEAD_DIM
WA_W = WA_HEADS * HEAD_DIM
WA_KV_W = WA_KV_HEADS * HEAD_DIM
Q_W = NA_W + WA_W
IN_W = Q_W + 2 * NA_W + 2 * WA_KV_W


def rms_norm_2(x, g):
    xf = x.astype(jnp.float32)
    y = xf * lax.rsqrt(jnp.mean(xf * xf, axis=-1, keepdims=True) + NORM_EPS)
    return (y * g.astype(jnp.float32)).astype(x.dtype)

def modulate(h, shift, scale):
    return h * (1 + scale) + shift

def ada_params(cond, w_ada, b_ada):
    m = jax.nn.silu(cond) @ w_ada + b_ada
    return m.reshape(m.shape[:-1] + (N_MOD, D_MODEL))

def swiglu_half_step(x, g, mod, j, w_up, w_down):
    h = modulate(rms_norm_2(x, g), mod[..., j, :], mod[..., j + 1, :])
    gt, up = jnp.split(h @ w_up, 2, axis=-1)
    return x + MACARON_W * mod[..., j + 2, :] * ((jax.nn.silu(gt) * up) @ w_down)

def heads(t):
    return t.reshape(t.shape[:-1] + (t.shape[-1] // HEAD_DIM, HEAD_DIM))

def axial_rope_tables(n_tokens):
    rot = HEAD_DIM // 2
    inv_freq = ROPE_BASE ** (-jnp.arange(0, rot, 2, dtype=jnp.float32) / rot)
    t = jnp.arange(n_tokens)
    row = (t // GRID_W).astype(jnp.float32)
    col = (t % GRID_W).astype(jnp.float32)
    ang = jnp.stack([row[:, None] * inv_freq, col[:, None] * inv_freq], axis=1)
    return jnp.cos(ang), jnp.sin(ang)

def apply_axial_rope(x, cos, sin):
    B, S, H, Dh = x.shape
    xr = x.reshape(B, S, H, 2, 2, Dh // 4)
    x1, x2 = xr[..., 0, :], xr[..., 1, :]
    c = cos[:, None].astype(x.dtype)
    s = sin[:, None].astype(x.dtype)
    out = jnp.stack([x1 * c - x2 * s, x2 * c + x1 * s], axis=-2)
    return out.reshape(B, S, H, Dh)

def context_self_attention(q, k, v, sink):
    B, C, Hq, Dh = q.shape
    Hkv = k.shape[2]
    G = Hq // Hkv
    qg = (q * Dh ** -0.5).reshape(B, C, Hkv, G, Dh)
    s = jnp.einsum('bqkgd,bckd->bkgqc', qg, k).astype(jnp.float32)
    if sink is not None:
        sink_col = jnp.broadcast_to(sink.astype(jnp.float32).reshape(1, Hkv, G, 1, 1), s.shape[:-1] + (1,))
        s = jnp.concatenate([s, sink_col], axis=-1)
    p = jax.nn.softmax(s, axis=-1)[..., :C].astype(v.dtype)
    out = jnp.einsum('bkgqc,bckd->bqkgd', p, v)
    return out.reshape(B, C, Hq * Dh)

def neighbourhood_attention(q, k, v, k_ctx, v_ctx, rpb):
    B, S, H, Dh = q.shape
    rows = S // GRID_W
    kh = min(NA_KH, rows)
    n_nb = kh * NA_KW
    qg = (q * Dh ** -0.5).reshape(B, rows, GRID_W, H, Dh)
    kg = k.reshape(B, rows, GRID_W, H, Dh)
    vg = v.reshape(B, rows, GRID_W, H, Dh)
    col = jnp.arange(GRID_W)
    c0 = jnp.clip(col - NA_KW // 2, 0, GRID_W - NA_KW)
    col_idx = c0[:, None] + jnp.arange(NA_KW)[None, :]
    dc = col_idx - col[:, None] + (NA_KW - 1)
    rpb32 = rpb.astype(jnp.float32)

    def one_row(r):
        r0 = jnp.clip(r - kh // 2, 0, rows - kh)
        q_r = lax.dynamic_index_in_dim(qg, r, axis=1, keepdims=False)
        k_rows = lax.dynamic_slice_in_dim(kg, r0, kh, axis=1)
        v_rows = lax.dynamic_slice_in_dim(vg, r0, kh, axis=1)
        k_win = k_rows[:, :, col_idx]
        v_win = v_rows[:, :, col_idx]
        dr = r0 + jnp.arange(kh) - r + (NA_KH - 1)
        bias = rpb32[:, dr[:, None, None], dc[None, :, :]].transpose(0, 2, 1, 3)
        s_nb = jnp.einsum('bqhd,biqjhd->bhqij', q_r, k_win).astype(jnp.float32) + bias[None]
        s_ctx = jnp.einsum('bqhd,bchd->bhqc', q_r, k_ctx).astype(jnp.float32)
        logits = jnp.concatenate([s_nb.reshape(B, H, GRID_W, n_nb), s_ctx], axis=-1)
        p = jax.nn.softmax(logits, axis=-1).astype(v.dtype)
        p_nb = p[..., :n_nb].reshape(B, H, GRID_W, kh, NA_KW)
        return (jnp.einsum('bhqij,biqjhd->bqhd', p_nb, v_win)
                + jnp.einsum('bhqc,bchd->bqhd', p[..., n_nb:], v_ctx))

    out = lax.map(one_row, jnp.arange(rows))
    return out.transpose(1, 0, 2, 3, 4).reshape(B, S, H * Dh)

def windowed_gqa_attention(q, k, v, k_ctx, v_ctx, sink):
    B, S, Hq, Dh = q.shape
    Hkv = k.shape[2]
    G = Hq // Hkv
    nb = S // WA_BLOCK
    n_loc = 3 * WA_BLOCK
    qb = (q * Dh ** -0.5).reshape(B, nb, WA_BLOCK, Hkv, G, Dh)
    pad = ((0, 0), (WA_BLOCK, WA_BLOCK), (0, 0), (0, 0))
    kp = jnp.pad(k, pad)
    vp = jnp.pad(v, pad)
    q_off = jnp.arange(WA_BLOCK)
    k_off = jnp.arange(n_loc) - WA_BLOCK
    band = jnp.abs(k_off[None, :] - q_off[:, None]) <= WA_WINDOW
    sink_col = jnp.broadcast_to(sink.astype(jnp.float32).reshape(1, Hkv, G, 1, 1), (B, Hkv, G, WA_BLOCK, 1))

    def one_block(i):
        q_i = lax.dynamic_index_in_dim(qb, i, axis=1, keepdims=False)
        k_i = lax.dynamic_slice_in_dim(kp, i * WA_BLOCK, n_loc, axis=1)
        v_i = lax.dynamic_slice_in_dim(vp, i * WA_BLOCK, n_loc, axis=1)
        k_pos = i * WA_BLOCK + k_off
        valid = band & ((k_pos >= 0) & (k_pos < S))[None, :]
        s_loc = jnp.einsum('bqkgd,bjkd->bkgqj', q_i, k_i).astype(jnp.float32)
        s_loc = jnp.where(valid, s_loc, NEG_INF_2)
        s_ctx = jnp.einsum('bqkgd,bckd->bkgqc', q_i, k_ctx).astype(jnp.float32)
        p = jax.nn.softmax(jnp.concatenate([s_loc, s_ctx, sink_col], axis=-1), axis=-1).astype(v.dtype)
        out = (jnp.einsum('bkgqj,bjkd->bqkgd', p[..., :n_loc], v_i)
               + jnp.einsum('bkgqc,bckd->bqkgd', p[..., n_loc:-1], v_ctx))
        return out.reshape(B, WA_BLOCK, Hq * Dh)

    out = lax.map(one_block, jnp.arange(nb))
    return out.transpose(1, 0, 2, 3).reshape(B, S, Hq * Dh)

def split_kv(p):
    o1, o2, o3 = NA_W, 2 * NA_W, 2 * NA_W + WA_KV_W
    return p[..., :o1], p[..., o1:o2], p[..., o2:o3], p[..., o3:]

def second_inputs(seed: int = 0) -> dict:
    key = jax.random.key(seed)
    ks = jax.random.split(key, 14)
    f32 = jnp.float32

    def nrm(k, shape, scale):
        return jax.random.normal(k, shape, f32) * scale

    return {
        "x": nrm(ks[0], (BATCH, SEQ, D_MODEL), 1.0),
        "c": nrm(ks[1], (BATCH, D_MODEL), 1.0),
        "ctx": nrm(ks[2], (BATCH, CTX_LEN, D_MODEL), 1.0),
        "c_ctx": nrm(ks[3], (D_MODEL,), 1.0),
        "w_ada": nrm(ks[4], (DEPTH, D_MODEL, N_MOD * D_MODEL), 0.5 * D_MODEL ** -0.5),
        "b_ada": nrm(ks[5], (DEPTH, N_MOD * D_MODEL), 0.02),
        "norm_g": 1.0 + nrm(ks[6], (DEPTH, 3, D_MODEL), 0.02),
        "w_ffn_up": nrm(ks[7], (DEPTH, 2, D_MODEL, 2 * D_FF_2), D_MODEL ** -0.5),
        "w_ffn_down": nrm(ks[8], (DEPTH, 2, D_FF_2, D_MODEL), D_FF_2 ** -0.5),
        "w_in": nrm(ks[9], (DEPTH, D_MODEL, IN_W), D_MODEL ** -0.5),
        "w_out": nrm(ks[10], (DEPTH, Q_W, D_MODEL), Q_W ** -0.5),
        "qk_norm_g": 1.0 + nrm(ks[11], (DEPTH, 4, HEAD_DIM), 0.02),
        "na_rpb": nrm(ks[12], (DEPTH, NA_HEADS, 2 * NA_KH - 1, 2 * NA_KW - 1), 0.1),
        "wa_sink": nrm(ks[13], (DEPTH, WA_HEADS), 0.5),
    }

def second_block(x, c, ctx, c_ctx, w_ada, b_ada, norm_g, w_ffn_up, w_ffn_down, w_in, w_out,
              qk_norm_g, na_rpb, wa_sink):
    S = x.shape[1]
    cos, sin = axial_rope_tables(S)
    h_ctx = ctx
    for l in range(DEPTH):
        last = l == DEPTH - 1
        mod_x = ada_params(c, w_ada[l], b_ada[l])[:, None]
        mod_c = ada_params(c_ctx, w_ada[l], b_ada[l])[None, None]

        x = swiglu_half_step(x, norm_g[l, 0], mod_x, 0, w_ffn_up[l, 0], w_ffn_down[l, 0])
        h_ctx = swiglu_half_step(h_ctx, norm_g[l, 0], mod_c, 0, w_ffn_up[l, 0], w_ffn_down[l, 0])

        hx = modulate(rms_norm_2(x, norm_g[l, 1]), mod_x[..., 3, :], mod_x[..., 4, :])
        hc = modulate(rms_norm_2(h_ctx, norm_g[l, 1]), mod_c[..., 3, :], mod_c[..., 4, :])
        px = hx @ w_in[l]
        pc = hc @ (w_in[l, :, Q_W:] if last else w_in[l])
        pc_kv = pc[..., -(IN_W - Q_W):]

        qa = rms_norm_2(heads(px[..., :NA_W]), qk_norm_g[l, 0])
        qb = rms_norm_2(heads(px[..., NA_W:Q_W]), qk_norm_g[l, 2])
        ka, va, kb, vb = split_kv(px[..., Q_W:])
        ka = rms_norm_2(heads(ka), qk_norm_g[l, 1])
        kb = rms_norm_2(heads(kb), qk_norm_g[l, 3])
        va, vb = heads(va), heads(vb)
        qb = apply_axial_rope(qb, cos, sin)
        kb = apply_axial_rope(kb, cos, sin)

        ka_c, va_c, kb_c, vb_c = split_kv(pc_kv)
        ka_c = rms_norm_2(heads(ka_c), qk_norm_g[l, 1])
        kb_c = rms_norm_2(heads(kb_c), qk_norm_g[l, 3])
        va_c, vb_c = heads(va_c), heads(vb_c)

        out_a = neighbourhood_attention(qa, ka, va, ka_c, va_c, na_rpb[l])
        out_b = windowed_gqa_attention(qb, kb, vb, kb_c, vb_c, wa_sink[l])
        x = x + mod_x[..., 5, :] * (jnp.concatenate([out_a, out_b], axis=-1) @ w_out[l])

        if not last:
            qa_c = rms_norm_2(heads(pc[..., :NA_W]), qk_norm_g[l, 0])
            qb_c = rms_norm_2(heads(pc[..., NA_W:Q_W]), qk_norm_g[l, 2])
            out_a_c = context_self_attention(qa_c, ka_c, va_c, None)
            out_b_c = context_self_attention(qb_c, kb_c, vb_c, wa_sink[l])
            h_ctx = h_ctx + mod_c[..., 5, :] * (jnp.concatenate([out_a_c, out_b_c], axis=-1) @ w_out[l])

        x = swiglu_half_step(x, norm_g[l, 2], mod_x, 6, w_ffn_up[l, 1], w_ffn_down[l, 1])
        if not last:
            h_ctx = swiglu_half_step(h_ctx, norm_g[l, 2], mod_c, 6, w_ffn_up[l, 1], w_ffn_down[l, 1])
    return x


def setup_inputs(seed=0):
    out = dict(first_inputs(seed))
    for name, value in second_inputs(seed + 1).items():
        if name != "x":
            out[name + "_2"] = value
    return out


def reference(
    x, norm_mix_g, w_in, conv_w, conv_b, conv_ln_g, conv_ln_b, moba_out_g, gla_gate_w,
    gla_gate_b, gla_out_g, w_out, norm_ffn_g, ffn_w_up, ffn_conv_w, ffn_conv_b, ffn_w_down,
    final_g, c_2, ctx_2, c_ctx_2, w_ada_2, b_ada_2, norm_g_2, w_ffn_up_2, w_ffn_down_2, w_in_2,
    w_out_2, qk_norm_g_2, na_rpb_2, wa_sink_2,
):
    x = first_block(
        x, norm_mix_g, w_in, conv_w, conv_b, conv_ln_g, conv_ln_b, moba_out_g, gla_gate_w,
        gla_gate_b, gla_out_g, w_out, norm_ffn_g, ffn_w_up, ffn_conv_w, ffn_conv_b, ffn_w_down,
        final_g,
    )
    return second_block(
        x, c_2, ctx_2, c_ctx_2, w_ada_2, b_ada_2, norm_g_2, w_ffn_up_2, w_ffn_down_2, w_in_2,
        w_out_2, qk_norm_g_2, na_rpb_2, wa_sink_2,
    )


_drawn_inputs = setup_inputs


def setup_inputs(seed=0):
    import zlib

    import numpy as np

    out = dict(_drawn_inputs(seed))
    spreads = {}
    factors = {'conv_b': 2.856,
     'conv_ln_b': 5.712,
     'ffn_conv_b': 2.914,
     'b_ada_2': 2.778,
     'norm_g_2': 8.0,
     'qk_norm_g_2': 8.0,
     'na_rpb_2': 8.0,
     'wa_sink_2': 8.0}
    for name, (base, spread) in spreads.items():
        noise = np.random.default_rng([zlib.crc32(name.encode()), seed]).standard_normal(out[name].shape)
        drawn = base * np.exp(spread * noise) if base else spread * noise
        out[name] = __import__('jax').numpy.asarray(drawn.astype(out[name].dtype))
    for name, factor in factors.items():
        out[name] = (out[name] * factor).astype(out[name].dtype)
    return out
```

```python
from contextlib import ExitStack

import numpy as np
import concourse.bass as bass
from concourse import mybir

F32 = mybir.dt.float32
F32R = mybir.dt.float32r
I32 = mybir.dt.int32
ALU = mybir.AluOpType
ACT = mybir.ActivationFunctionType
AX = mybir.AxisListType

P = 128
D = 1024
KT = D // P
SEQ = 256
CTX = 256
DEPTH = 2
FF = 2816
FT = FF // P
PAIRS = FT // 2
TAPS = 31
HALO = TAPS - 1
CHUNK = 32
NCH = SEQ // CHUNK
RING = 4
AHEAD = 3
UNIT = 1024
ADA_RING = 2
N_MOD = 9
MODS = N_MOD * KT
ADA_UNITS = DEPTH * MODS
HALVINGS = 10
EPS = 1e-6
LN_EPS = 1e-5
BIG = -1e30
MIX_COLS = 2832
G_COL = 2304

_par = {}
_n = 0


def _col(name, n):
    global _n
    _par[name] = _n
    _n += n


for _l in range(DEPTH):
    _col(f"mix_g{_l}", 8)
    _col(f"ffn_g{_l}", 8)
    _col(f"conv_w{_l}", 2 * TAPS)
    _col(f"conv_b{_l}", 2)
    _col(f"ln_g{_l}", 2)
    _col(f"ln_b{_l}", 2)
    _col(f"moba_g{_l}", 2)
    _col(f"gate_b{_l}", 2)
    _col(f"gla_g{_l}", 4)
    _col(f"ffn_conv{_l}", 16 * PAIRS)
    _col(f"norm_g{_l}", 24)
    _col(f"b_ada{_l}", MODS)
    _col(f"qk_g{_l}", 4)
    _col(f"sink{_l}", 8)
    _col(f"gate_w{_l}", 256)
    _col(f"rpb{_l}", 48)
_col("final_g", 8)
N_PAR = _n
_n = 0
for _name, _k in (("ident", 128), ("ones", 2), ("mean256", 128), ("two", 2), ("causal", 512), ("band", 256),
                  ("colmask", 64), ("reset", 256), ("cos", 256), ("sin", 256), ("hot", 191)):
    _col("c_" + _name, _k)
N_CONST = _n


class Stage:

    def __init__(self, kind, n_units, at, l=0, N=SEQ, blk=0, which=0, m0=0, pairs=0, ffn=0, gate=None, n=0,
                 last=False):
        self.kind, self.n_units = kind, n_units
        self.l, self.N, self.blk, self.which = l, N, blk, which
        self.m0, self.pairs, self.ffn, self.gate = m0, pairs, ffn, gate
        self.n, self.last = n, last
        self.u = at["u"]
        self.tok = at["tok"]
        self.h = at["h"]
        self.rs = at["rs"]
        self.sq = at["sq"]
        self.sa = at["sa"]
        self.nm = at["nm"]
        self.ia = at["ia"]
        self.hid = at["hid"]
        self.grp = at["grp"]
        self.sunk = at["sunk"]


class Group:

    def __init__(self, i, tok, nk, q, k, v, scale=1.0, mask=None, sink=None, sinks=None, si=0, out=None, yi=0,
                 dst=None):
        self.i, self.tok, self.nk, self.scale = i, tok, nk, scale
        self.q, self.k, self.v, self.mask = q, k, v, mask
        self.sink, self.sinks, self.si = sink, sinks, si
        self.out, self.yi, self.dst = out, yi, dst


class Counter:
    def __init__(self):
        self.steps = 0
        self.last = None


def make_plan():
    c = dict(u=0, tok=0, h=0, rs=0, sq=0, sa=0, nm=0, ia=0, hid=0, grp=0, sunk=0)
    stages = []

    def add(kind, units=0, more=(), **kw):
        stages.append(Stage(kind, units, c, **kw))
        c["u"] += units
        for name, n in dict(more).items():
            c[name] += n

    def ffn(l, N, blk, which=0, gate=None):
        groups = [PAIRS] if N == SEQ else [6, 5]
        m0 = 0
        for g in groups:
            add("up", units=4 * g, more=dict(tok=g, hid=g), l=l, N=N, blk=blk, m0=m0, pairs=g, ffn=which)
            add("down", units=2 * g, more=dict(tok=2), l=l, N=N, blk=blk, m0=m0, pairs=g, gate=gate, ffn=which)
            m0 += g

    def norm(l, N, blk, which):
        if blk == 2:
            add("mods", l=l, which=which)
        add("norm", more=dict(tok=1, h=8, rs=1, sq=1, sa=1, nm=1), l=l, N=N, blk=blk, which=which)

    for l in range(DEPTH):
        norm(l, SEQ, 1, 0)
        add("in1", units=23, more=dict(tok=6, ia=1), l=l)
        add("att1", more=dict(tok=11, h=8, rs=3, sq=3, grp=4), l=l)
        add("out", units=8, more=dict(tok=2), l=l, N=SEQ, blk=1)
        norm(l, SEQ, 1, 1)
        ffn(l, SEQ, 1)
    add("final", more=dict(tok=1, rs=1, sq=1, sa=1), l=0, N=SEQ, blk=1)
    for l in range(DEPTH):
        last = l == DEPTH - 1
        n2 = SEQ if last else SEQ + CTX
        norm(l, SEQ + CTX, 2, 0)
        ffn(l, SEQ + CTX, 2, 0, 0)
        norm(l, SEQ + CTX, 2, 1)
        add("in2", units=18, more=dict(tok=5, ia=4), l=l, last=last)
        n = 4 * 2 * 2 * (n2 // SEQ)
        add("att2", more=dict(tok=1 + 4 + 8 + n, rs=1, grp=n, sunk=n // 2), l=l, last=last)
        add("out", units=8, more=dict(tok=2), l=l, N=n2, blk=2, gate=1)
        norm(l, n2, 2, 2)
        ffn(l, n2, 2, 1, 2)
    return stages, c


PLAN, TOTAL = make_plan()

QB_ORDER = np.concatenate([np.arange(64) + 64 * h for t in range(4) for h in (t, t + 4)])


def bcast_last(ap, n):
    return ap.unsqueeze(2).to_broadcast([ap.shape[0], ap.shape[1], n])


def bcast_mid(ap, n):
    return ap.unsqueeze(1).to_broadcast([ap.shape[0], n, ap.shape[1]])


def flat(ap):
    return ap.rearrange("p a b -> p (a b)")


def qk_cols(st):
    q_tiles = (SEQ if st.last else SEQ + CTX) // P
    return [(t, tt) for t in range(8) for tt in range(q_tiles)] + [(t, tt) for t in range(8, 13) for tt in range(4)]


def up_loop(eng, st, split, post):
    for j in range(4):
        split(st.u + j)

    def macro(k, more):
        for j in range(4):
            split(st.u + 4 * (1 + k) + j, more)
            post(j, st.tok + k, k + more)

    turns = (st.pairs - 1) // 2
    if turns > 1:
        with eng.Fori(0, turns) as i:
            for k in range(2):
                macro(k, 2 * i)
    else:
        for k in range(2 * turns):
            macro(k, 0)
    for k in range(2 * turns, st.pairs - 1):
        macro(k, 0)
    for j in range(4):
        post(j, st.tok + st.pairs - 1, st.pairs - 1)


class Semaphores:

    def __init__(self, new):
        self.loaded = new("loaded")
        self.at_zero = new("at_zero")
        self.cond_ready = new("cond_ready")
        self.stored = new("stored")
        self.w_hi = new("w_hi")
        self.w_lo = new("w_lo")
        self.units_done = new("units_done")
        self.mod_halves = new("mod_halves")
        self.mod_sums = new("mod_sums")
        self.evac = new("evac")
        self.gain_ready = new("gain_ready")
        self.squared_a = new("squared_a")
        self.squared = new("squared")
        self.stats = new("stats")
        self.var = new("var")
        self.log_var = new("log_var")
        self.rstd0 = new("rstd0")
        self.rstd = new("rstd")
        self.rstd_b = new("rstd_b")
        self.scaled = new("scaled")
        self.h_hi = new("h_hi")
        self.h_ready = new("h_ready")
        self.biased = new("biased")
        self.conv1 = new("conv1")
        self.silued = new("silued")
        self.hid_f32 = new("hid_f32")
        self.hid_hi = new("hid_hi")
        self.hid_ready = new("hid_ready")
        self.scores = new("scores")
        self.negmax = new("negmax")
        self.sink_exp = new("sink_exp")
        self.probs_exp = new("probs_exp")
        self.probs = new("probs")
        self.probsT = new("probsT")
        self.probsT_sb = new("probsT_sb")
        self.pv = new("pv")
        self.y_hi = new("y_hi")
        self.sig = new("sig")
        self.tap = new("tap")
        self.in_act = new("in_act")
        self.gate_logits = new("gate_logits")
        self.gate_min = new("gate_min")
        self.gate_abs = new("gate_abs")
        self.gate_e = new("gate_e")
        self.gate_l = new("gate_l")
        self.gate_d = new("gate_d")
        self.gate_exps = new("gate_exps")
        self.gla_in = new("gla_in")
        self.kdT = new("kdT")
        self.attnT = new("attnT")
        self.kdT_sb = new("kdT_sb")
        self.attn_sb = new("attn_sb")
        self.d_state = new("d_state")
        self.state = new("state")
        self.gla_o = new("gla_o")
        self.mu = new("mu")
        self.centered = new("centered")
        self.ln_out = new("ln_out")
        self.ln_act = new("ln_act")
        self.mix_y = new("mix_y")
        self.mix_hi = new("mix_hi")
        self.dve_step = new("dve_step")
        self.qk_rb = new("qk_rb")
        self.roped = new("roped")
        self.bias_ps = new("bias_ps")
        self.raw_in = [new(f"raw_in{i}") for i in range(RING)]
        self.ada_in = [new(f"ada_in{i}") for i in range(ADA_RING)]


def build_kernel(nc, xT, ctxT, wstream, adastream, par, const, imask, cond, outT):
    with ExitStack() as ctx:
        def sb(name, shape, dt=F32):
            return ctx.enter_context(nc.sbuf_tensor(name, shape, dt))

        X = sb("X", [P, KT, 512])
        H_hi = sb("H_hi", [P, KT, 512], F32R)
        H_lo = sb("H_lo", [P, KT, 512], F32R)
        W_raw = sb("W_raw", [P, RING, UNIT])
        W_hi = sb("W_hi", [P, RING, UNIT], F32R)
        W_lo = sb("W_lo", [P, RING, UNIT], F32R)
        A_raw = sb("A_raw", [P, ADA_RING, UNIT])
        PROD = sb("PROD", [P, 2, UNIT])
        PAR = sb("PAR", [P, N_PAR])
        CON = sb("CON", [P, N_CONST])
        MASKI = sb("MASKI", [P, P], I32)
        MOD = sb("MOD", [P, DEPTH, MODS, 2])
        GAIN = sb("GAIN", [P, 3, KT, 2])
        GATE = sb("GATE", [P, 3, KT, 2])
        SC = sb("SC", [P, 2, D])
        AT = sb("AT", [P, 8, P])
        V_ = sb("V_", [P, 112])
        L_ = sb("L_", [P, 112])
        R0 = sb("R0", [P, 112])
        T_ = sb("T_", [P, 112])
        RS = sb("RS", [P, 112])
        NM = sb("NM", [P, 2, 2])
        SM = sb("SM", [P, 2, 2])
        RI = sb("RI", [P, 2, 2])
        ES = sb("ES", [P, 2, 2])
        ARENA = 64 * 1024
        base = (nc.sbuf_base + 31) // 32 * 32
        arena = sb("arena", [P, ARENA // 4])

        def at(name, off, shape, dt=F32):
            size = 4 * int(np.prod(shape[1:]))
            assert off + size <= ARENA, (name, off, size)
            return nc.alloc_sbuf_tensor_at(name, shape, dt, offset=base + off)

        K = 1024
        HID_hi = at("HID_hi", 0, [P, 12 * 512], F32R)
        HID_lo = at("HID_lo", 24 * K, [P, 12 * 512], F32R)
        U = at("U", 48 * K, [P, 4, SEQ])
        SG = at("SG", 52 * K, [P, 2 * 512])
        HF = at("HF", 56 * K, [P, 2 * 512])
        SQ = at("SQ", 48 * K, [P, KT, 512])
        TMP = at("TMP", 16 * K, [P, KT, 512])
        Q = at("Q", 0, [P, 8, 512])
        KM = at("KM", 16 * K, [P, 5, 512])
        V = at("V", 26 * K, [P, 4, 640])
        PR = at("PR", 36 * K, [P, 2, 2, 512])
        PTS = at("PTS", 44 * K, [P, 2, 2, 512])
        SQ2 = at("SQ2", 36 * K, [P, 13, 512])
        BT = at("BT", 52 * K, [P, 48, 64])
        ROT = at("ROT", 36 * K, [P, 5, SEQ])
        QG = at("QG", 4 * K, [P, 2, SEQ])
        KG = at("KG", 6 * K, [P, 2, SEQ])
        KD = at("KD", 8 * K, [P, 2, SEQ])
        OM = at("OM", 10 * K, [P, 2, SEQ])
        AC = at("AC", 12 * K, [P, 2, SEQ])
        SGM = at("SGM", 14 * K, [P, 2, SEQ])
        HC = at("HC", 52 * K, [P, 2, HALO + SEQ])
        GG = at("GG", 55 * K, [P, SEQ])
        VG = at("VG", 56 * K, [P, 2, 512])
        SR = at("SR", 60 * K, [P, 4, SEQ])
        ST = at("ST", 36 * K, [P, NCH, 2, P])
        EG = at("EG", 30 * K, [P, 2, SEQ])
        EN = at("EN", 32 * K, [P, 2, SEQ])
        ED = at("ED", 34 * K, [P, 2, SEQ])
        Z = at("Z", 20 * K, [P, 2, SEQ])
        LA = at("LA", 14 * K, [P, 2, SEQ])
        GS = at("GS", 22 * K, [P, 2, SEQ])
        KDT = at("KDT", 44 * K, [P, 2, SEQ])
        OG = at("OG", 22 * K, [P, 4, SEQ])
        Y = at("Y", 0, [P, 8, SEQ])
        TMPA = at("TMPA", 52 * K, [P, 2, SEQ])
        SQA = at("SQA", 44 * K, [P, 8, SEQ])
        psum = [ctx.enter_context(nc.psum_tensor(f"half{i}", [P, 4, 512], F32)) for i in range(2)]

        def ps(tok):
            return psum[tok % 2]

        S = Semaphores(lambda name: ctx.enter_context(nc.semaphore(name)))
        raw_in, ada_in = S.raw_in, S.ada_in

        def con(name, n):
            o = _par["c_" + name]
            return CON[:, o:o + n]

        def par1(name, i=0, rows=slice(0, P)):
            o = _par[name] + i
            return PAR[rows, o:o + 1]

        ident = con("ident", 128)
        N_LOADS = 6

        def gain_of(st, kt, half):
            if st.blk == 1:
                return par1(("mix_g", "ffn_g")[st.which] + str(st.l), kt)
            return GAIN[:, st.which, kt, half:half + 1]

        def shift_of(st, kt, half):
            return MOD[:, st.l, 3 * st.which * KT + kt, half:half + 1]

        def wait(eng, sem, value):
            if isinstance(value, int) and value <= 0:
                return
            eng.wait_ge(sem, value)

        def groups1(st):
            out = []
            causal = con("causal", 512)
            for t in range(2):
                for qt in range(2):
                    out.append(Group(
                        i=st.grp + len(out), tok=st.tok + 1 + len(out), nk=SEQ, scale=0.125,
                        q=Q[:, t, P * qt:P * qt + P], k=KM[:, t, 0:SEQ],
                        v=lambda h, kb, t=t: V[:, kb, 64 * (2 * t + h):64 * (2 * t + h) + 64],
                        mask=bcast_mid(causal[:, SEQ * qt:SEQ * qt + SEQ], 2), dst=OM[:, t, P * qt:P * qt + P]))
            return out

        def groups2(st):
            out = []
            window = con("causal", 512)[:, SEQ:2 * SEQ], con("band", 256)
            bias = BT[:, :, :].rearrange("p (h e) c -> p h (e c)", e=6)
            for qt in range(2 if st.last else 4):
                for wa in range(2):
                    for t in range(4):
                        n = len(out)
                        kt = 4 if wa else t
                        nk, k0 = (SEQ + CTX, 0) if qt < 2 else (CTX, SEQ)
                        g = Group(i=st.grp + n, tok=st.tok + 13 + n, yi=st.grp + n - 4 * DEPTH, nk=nk,
                                  q=Q[:, 4 * wa + t, P * qt:P * qt + P], k=KM[:, kt, k0:k0 + nk],
                                  v=lambda h, kb, k0=k0, v0=512 if wa else P * t:
                                  V[:, k0 // P + kb, v0 + 64 * h:v0 + 64 * h + 64],
                                  out=(slice(0, P), 4 * wa + t, slice(P * qt, P * qt + P)))
                        if wa:
                            o = _par[f"sink{st.l}"] + 2 * t
                            g.sinks = PAR[:, o:o + 2]
                            g.sink = lambda h, o=o: PAR[:, o + h:o + h + 1]
                            g.si = st.sunk + sum(x.sink is not None for x in out)
                            if qt < 2:
                                g.mask = bcast_mid(window[qt], 2)
                        elif qt < 2:
                            e = 64 * (2 - 2 * qt)
                            g.mask = bias[:, 2 * t:2 * t + 2, e:e + SEQ]
                        out.append(g)
            return out

        def halves(N):
            return range(N // SEQ)

        block = ctx.enter_context(nc.Block())

        @block.sync
        def _(sp):
            sp.dma_start(X[:, :, 0:SEQ], xT).then_inc(S.loaded, 16)
            sp.dma_start(CON[:, :], const).then_inc(S.loaded, 16)
            sp.dma_start(PAR[:, :], par).then_inc(S.loaded, 16)
            sp.dma_start(X[:, :, SEQ:512], ctxT).then_inc(S.loaded, 16)
            sp.dma_start(MASKI[:, :], imask).then_inc(S.loaded, 16)
            sp.dma_start(SC[:, :, :], cond).then_inc(S.loaded, 16)

            def load(slot, unit, lo_needed):
                wait(sp, S.w_lo, lo_needed)
                sp.dma_start(W_raw[:, slot, :], wstream[bass.ds(unit * P, P), :]).then_inc(raw_in[slot], 16)

            for u in range(RING):
                load(u, u, 0)
            full = TOTAL["u"] // RING
            with sp.Fori(1, full) as i:
                for j in range(RING):
                    load(j, i * RING + j, i * RING + j - RING + 1)
            for u in range(full * RING, TOTAL["u"]):
                load(u % RING, u, u - RING + 1)
            sp.wait_ge(S.evac, TOTAL["tok"])
            sp.dma_start(outT, X[:, :, 0:SEQ]).then_inc(S.stored, 16)
            sp.wait_ge(S.stored, 16)

        @block.gpsimd
        def _(pool):
            for a in range(ADA_RING):
                pool.dma_start(A_raw[:, a, :], adastream[P * a:P * a + P, :]).then_inc(ada_in[a], 16)
            pool.memset(AT[:, :, :], 0.0).then_inc(S.at_zero, 1)

            sums = MOD[:, :, :, :].rearrange("p l t b -> p (l t b)")

            def column_tile(slot, l, t, i, row):
                n = t + (MODS * l + 1)
                pool.wait_ge(ada_in[slot], 16 * i)
                pool.tensor_tensor(PROD[:, :, :], bcast_mid(A_raw[:, slot, :], 2), SC[:, :, :], ALU.mult)\
                    .then_inc(S.mod_halves, 1)
                w = D
                for k in range(HALVINGS):
                    w //= 2
                    pool.wait_ge(S.mod_halves, HALVINGS * n - (HALVINGS - 1 - k))
                    if k < HALVINGS - 1:
                        pool.tensor_tensor(PROD[:, :, 0:w], PROD[:, :, 0:w], PROD[:, :, w:2 * w], ALU.add)\
                            .then_inc(S.mod_halves, 1)
                pool.tensor_tensor(sums[:, bass.ds(2 * MODS * l + 2 * t, 2)], PROD[:, :, 0], PROD[:, :, 1], ALU.add)\
                    .then_inc(S.mod_sums, 1)
                pool.wait_ge(S.mod_sums, n)
                if row is not None:
                    pool.dma_start(A_raw[:, slot, :], adastream[row, :]).then_inc(ada_in[slot], 16)

            pool.wait_ge(S.cond_ready, 1)
            for l in range(DEPTH):
                first = MODS // ADA_RING * l
                turns = MODS // ADA_RING - (1 if l == DEPTH - 1 else 0)
                with pool.Fori(0, turns) as i:
                    for j in range(ADA_RING):
                        t = i * ADA_RING + j
                        column_tile(j, l, t, i + (first + 1),
                                    bass.ds((t + (MODS * l + ADA_RING)) * P, P))
                if l == DEPTH - 1:
                    for j in range(ADA_RING):
                        column_tile(j, l, MODS - ADA_RING + j, first + turns + 1, None)

        @block.tensor
        def _(pe):
            def three(out, wl, wh, xl, xh, start, stop):
                pe.matmul(out, wl, xh, start=start, stop=False, skip_group_check=True)
                pe.matmul(out, wh, xl, start=False, stop=False, skip_group_check=True)
                return pe.matmul(out, wh, xh, start=False, stop=stop, skip_group_check=True)

            def open_token(tok):
                wait(pe, S.evac, tok - 1)

            def feat_unit(ub, m, tok, q, N, h_wait):
                slot = (ub) % RING
                pe.wait_ge(S.w_lo, ub + 1 + 4 * m)
                for t in range(2):
                    for k in range(4):
                        kt = 4 * (q % 2) + k
                        if h_wait is not None:
                            wait(pe, S.h_ready, h_wait(kt))
                        c = slice(256 * k + 128 * t, 256 * k + 128 * t + 128)
                        mm = three(ps(tok)[:, 2 * (q // 2) + t, 0:N], W_lo[:, slot, c], W_hi[:, slot, c],
                                   H_lo[:, kt, 0:N], H_hi[:, kt, 0:N], kt == 0, kt == KT - 1)
                mm.then_inc(S.units_done, 1)

            def feat_macro(ub, m, tok, N, h_wait=None):
                open_token(tok)
                for q in range(4):
                    feat_unit(ub + q, m, tok, q, N, h_wait if q < 2 else None)

            def token_macro(ub, tok, N, width):
                for q in range(2 * width):
                    slot = (ub + q) % RING
                    pe.wait_ge(S.w_lo, ub + q + 1)
                    for tt in range(N // P):
                        for k in range(4):
                            kt = 4 * (q % 2) + k
                            o = (q // 2) * 256
                            three_t(ps(tok)[:, tt, o:o + 256], kt, slice(P * tt, P * tt + P), slot,
                                    slice(256 * k, 256 * k + 256))
                    last_of_unit()

            product = Counter()

            def three_t(out, kt, tk, slot, w, start=None, stop=None):
                start = (kt == 0) if start is None else start
                stop = (kt == KT - 1) if stop is None else stop
                pe.matmul(out, H_lo[:, kt, tk], W_hi[:, slot, w], start=start, stop=False, skip_group_check=True)
                pe.matmul(out, H_hi[:, kt, tk], W_lo[:, slot, w], start=False, stop=False, skip_group_check=True)
                product.last = pe.matmul(out, H_hi[:, kt, tk], W_hi[:, slot, w], start=False, stop=stop,
                                         skip_group_check=True)

            def last_of_unit():
                product.last.then_inc(S.units_done, 1)

            def stats(tok, cols, rhs, width):
                for c, blocks in enumerate(cols):
                    for i, b in enumerate(blocks):
                        mm = pe.matmul(ps(tok)[:, 0, width * c:width * c + width], b, rhs,
                                       start=(i == 0), stop=(i == len(blocks) - 1), skip_group_check=True)
                mm.then_inc(S.stats, 1)

            def spread(tok, st_rs, outs):
                pe.wait_ge(S.rstd, st_rs + 1)
                for out, src, rep in outs:
                    if rep == P:
                        mm = pe.transpose(out, src.to_broadcast([P, P]), ident)
                    for h in range(2 if rep == 64 else 0):
                        mm = pe.matmul(out[64 * h:64 * h + 64], src[:, h:h + 1].to_broadcast([P, 64]), ident,
                                       start=True, stop=True, skip_group_check=True)
                return mm

            def norm(st):
                tok = st.tok
                tts = st.N // P
                open_token(tok)
                pe.wait_ge(S.squared_a, st.sa + 1)
                for kt in range(KT):
                    if kt == KT // 2:
                        pe.wait_ge(S.squared, st.sq + 1)
                    for tt in range(tts):
                        mm = pe.matmul(ps(tok)[:, 0, tt:tt + 1], SQ[:, kt, P * tt:P * tt + P], con("ones", 1),
                                       start=(kt == 0 and tt == 0), stop=(kt == KT - 1), skip_group_check=True)
                mm.then_inc(S.stats, 1)
                mm = spread(tok, st.rs, [(ps(tok)[:, 1, P * tt:P * tt + P], RS[:, tt:tt + 1], P)
                                         for tt in range(tts)])
                mm.then_inc(S.rstd_b, 1)

            def in1(st):
                tok = st.tok
                hw = lambda kt: st.h - 8 + kt + 1
                feat_macro(st.u, 0, tok, SEQ, hw)
                feat_macro(st.u + 4, 0, tok + 1, SEQ)
                open_token(tok + 2)
                token_macro(st.u + 8, tok + 2, SEQ, 1)
                ub = st.u + 10
                pe.wait_ge(S.w_lo, ub + 1)
                for kt in range(KT):
                    c = slice(P * kt, P * kt + P)
                    mm = three(ps(tok + 2)[:, 2, 0:SEQ], W_lo[:, ub % RING, c], W_hi[:, ub % RING, c],
                               H_lo[:, kt, 0:SEQ], H_hi[:, kt, 0:SEQ], kt == 0, kt == KT - 1)
                mm.then_inc(S.units_done, 1)
                feat_macro(st.u + 11, 0, tok + 3, SEQ)
                open_token(tok + 4)
                token_macro(st.u + 15, tok + 4, SEQ, 2)
                feat_macro(st.u + 19, 0, tok + 5, SEQ)

            def scores(g):
                open_token(g.tok)
                for h in range(2):
                    b = slice(64 * h, 64 * h + 64)
                    mm = pe.matmul(ps(g.tok)[:, h, 0:g.nk], g.q[b], g.k[b], start=True, stop=True,
                                   skip_group_check=True)
                mm.then_inc(S.scores, 1)

            def probs_t(g):
                pe.wait_ge(S.probs, g.i + 1)
                for h in range(2):
                    for kb in range(g.nk // P):
                        mm = pe.transpose(ps(g.tok)[:, 2 + h, P * kb:P * kb + P],
                                          PR[:, g.i % 2, h, P * kb:P * kb + P], ident)
                mm.then_inc(S.probsT, 1)

            def weighted(g):
                pe.wait_ge(S.probsT_sb, g.i + 1)
                for h in range(2):
                    n = g.nk // P
                    for kb in range(n):
                        mm = pe.matmul(ps(g.tok)[64 * h:64 * h + 64, 0, 0:P], g.v(h, kb),
                                       PTS[:, g.i % 2, h, P * kb:P * kb + P], start=(kb == 0), stop=(kb == n - 1),
                                       skip_group_check=True)
                mm.then_inc(S.pv, 1)

            def groups(gs):
                scores(gs[0])
                for i, g in enumerate(gs):
                    probs_t(g)
                    if i + 1 < len(gs):
                        scores(gs[i + 1])
                    weighted(g)

            def att1(st):
                l, tok = st.l, st.tok
                open_token(tok)
                pe.wait_ge(S.evac, tok)
                for t in range(2):
                    o = _par[f"gate_w{l}"] + P * t
                    mm = pe.matmul(ps(tok)[:, 0, SEQ * t:SEQ * t + SEQ], PAR[0:16, o:o + P], GG[0:16, :],
                                   start=True, stop=True, skip_group_check=True)
                mm.then_inc(S.gate_logits, 1)
                groups(groups1(st))
                tok += 5
                open_token(tok)
                pe.wait_ge(S.gla_in, l + 1)
                for tt in range(2):
                    for t in range(2):
                        mm = pe.transpose(ps(tok)[:, 0, SEQ * tt + P * t:SEQ * tt + P * t + P],
                                          KD[:, t, P * tt:P * tt + P], ident)
                mm.then_inc(S.kdT, 1)
                for tt in range(2):
                    for pair in range(2):
                        for par_ in range(2):
                            b = slice(64 * par_, 64 * par_ + 64)
                            tk = slice(P * tt, P * tt + P)
                            c = P * (2 * tt + pair)
                            mm = pe.matmul(ps(tok)[:, 1 + par_, c:c + P], KG[b, pair, tk], QG[b, pair, tk],
                                           start=True, stop=True, skip_group_check=True)
                mm.then_inc(S.attnT, 1)
                tok += 1
                open_token(tok)
                pe.wait_ge(S.kdT_sb, l + 1)
                for c in range(NCH - 1):
                    r = slice(CHUNK * (c % 4), CHUNK * (c % 4) + CHUNK)
                    for h in range(4):
                        o = (c // 4) * 256 + (h // 2) * 128
                        mm = pe.matmul(ps(tok)[64 * (h % 2):64 * (h % 2) + 64, c % 4, o:o + P],
                                       KDT[r, c // 4, 64 * h:64 * h + 64], VG[r, c // 4, P * h:P * h + P],
                                       start=True, stop=True, skip_group_check=True)
                mm.then_inc(S.d_state, 1)
                tok += 1
                open_token(tok)
                pe.wait_ge(S.attn_sb, l + 1)
                pe.wait_ge(S.state, 16 * (l + 1))
                for h in range(4):
                    b = slice(64 * (h % 2), 64 * (h % 2) + 64)
                    for tt in range(2):
                        o = (h // 2) * SEQ + tt * P
                        pe.matmul(ps(tok)[:, h % 2, o:o + P], VG[:, tt, P * h:P * h + P],
                                  AT[:, 4 * (h % 2) + 2 * tt + h // 2, :], start=True, stop=False,
                                  skip_group_check=True)
                        for c in range(4 * tt, 4 * tt + 4):
                            if c == 0:
                                continue
                            o2 = (h // 2) * SEQ + c * CHUNK
                            mm = pe.matmul(ps(tok)[:, h % 2, o2:o2 + CHUNK], ST[b, c, h // 2, :],
                                           QG[b, h // 2, CHUNK * c:CHUNK * c + CHUNK], start=False,
                                           stop=(c == 4 * tt + 3), skip_group_check=True)
                mm.then_inc(S.gla_o, 1)
                tok += 1
                open_token(tok)
                pe.wait_ge(S.tap, 2 * TAPS * (l + 1))
                for t in range(2):
                    mm = pe.matmul(ps(tok)[:, 2, 0:SEQ], con("mean256", 128), AC[:, t, :], start=(t == 0),
                                   stop=(t == 1), skip_group_check=True)
                mm.then_inc(S.mu, 1)
                pe.wait_ge(S.squared, st.sq + 1)
                stats(tok, [[SQA[:, t, P * tt:P * tt + P] for t in range(2)] for tt in range(2)],
                      con("ones", 1), 1)
                mm = spread(tok, st.rs, [(ps(tok)[:, 1, P * tt:P * tt + P], RS[:, tt:tt + 1], P)
                                         for tt in range(2)])
                mm.then_inc(S.rstd_b, 1)
                tok += 1
                open_token(tok)
                pe.wait_ge(S.squared, st.sq + 2)
                stats(tok, [[SQA[:, 2 + t, P * tt:P * tt + P]] for t in range(2) for tt in range(2)],
                      con("two", 2), 2)
                mm = spread(tok, st.rs + 1, [(ps(tok)[:, 1, SEQ * t + P * tt:SEQ * t + P * tt + P],
                                              RS[:, 4 * t + 2 * tt:4 * t + 2 * tt + 2], 64)
                                             for t in range(2) for tt in range(2)])
                mm.then_inc(S.rstd_b, 1)
                tok += 1
                open_token(tok)
                pe.wait_ge(S.squared, st.sq + 3)
                stats(tok, [[SQA[:, 4 + t, P * tt:P * tt + P]] for t in range(4) for tt in range(2)],
                      con("ones", 1), 1)
                mm = spread(tok, st.rs + 2, [(ps(tok)[:, 1 + t // 2, SEQ * (t % 2) + P * tt:SEQ * (t % 2) + P * tt + P],
                                              RS[:, 2 * t + tt:2 * t + tt + 1], P)
                                             for t in range(4) for tt in range(2)])
                mm.then_inc(S.rstd_b, 1)

            def out_proj(st):
                wait(pe, S.h_ready, st.h)
                pe.wait_ge(S.evac, st.tok)
                for m in range(2):
                    feat_macro(st.u + 4 * m, 0, st.tok + m, st.N)

            def up(st):
                hw = lambda kt: st.h - 8 + kt + 1

                def macro(m_tok, ub, m, evac_base):
                    wait(pe, S.evac, evac_base)
                    for q in range(4):
                        feat_unit(ub + q, m, m_tok, q, st.N, None)

                open_token(st.tok)
                for q in range(4):
                    feat_unit(st.u + q, 0, st.tok, q, st.N, hw if q < 2 else None)
                rest = st.pairs - 1
                if rest // 2 > 1:
                    with pe.Fori(0, rest // 2) as i:
                        for b in range(2):
                            macro(st.tok + 1 + b, st.u + 4 * (1 + b), 2 * i, st.tok + b + 2 * i)
                else:
                    for i in range(rest // 2):
                        for b in range(2):
                            macro(st.tok + 1 + b, st.u + 4 * (1 + b), 2 * i, st.tok + b + 2 * i)
                for m in range(1 + 2 * (rest // 2), st.pairs):
                    macro(st.tok + m, st.u + 4 * m, 0, st.tok + m - 1)

            def down(st):
                for hf in range(2):
                    tok = st.tok + hf
                    open_token(tok)
                    for j in range(st.pairs):
                        u = st.u + hf * st.pairs + j
                        pe.wait_ge(S.w_lo, u + 1)
                        pe.wait_ge(S.hid_ready, st.hid - st.pairs + j + 1)
                        for k in range(2):
                            for t in range(4):
                                c = slice(512 * k + P * t, 512 * k + P * t + P)
                                x = slice((2 * j + k) * st.N, (2 * j + k + 1) * st.N)
                                mm = three(ps(tok)[:, t, 0:st.N], W_lo[:, u % RING, c], W_hi[:, u % RING, c],
                                           HID_lo[:, x], HID_hi[:, x], j + k == 0, j == st.pairs - 1 and k == 1)
                        mm.then_inc(S.units_done, 1)

            def in2(st):
                nq = SEQ if st.last else 512
                hw = lambda kt: st.h - 8 + kt + 1
                feat_macro(st.u, 0, st.tok, nq, hw)
                feat_macro(st.u + 4, 0, st.tok + 1, nq)
                feat_macro(st.u + 8, 0, st.tok + 2, 512)
                open_token(st.tok + 3)
                token_macro(st.u + 12, st.tok + 3, 512, 2)
                tok = st.tok + 4
                open_token(tok)
                for q in range(2):
                    u = st.u + 16 + q
                    pe.wait_ge(S.w_lo, u + 1)
                    for k in range(4):
                        kt = 4 * q + k
                        c = slice(256 * k, 256 * k + P)
                        three(ps(tok)[:, 0, :], W_lo[:, u % RING, c], W_hi[:, u % RING, c],
                              H_lo[:, kt, :], H_hi[:, kt, :], kt == 0, kt == KT - 1)
                    for tt in range(4):
                        for k in range(4):
                            kt = 4 * q + k
                            three_t(ps(tok)[:, 1, P * tt:P * tt + P], kt, slice(P * tt, P * tt + P), u % RING,
                                    slice(256 * k + P, 256 * k + 256), start=(kt == 0 and tt == 0))
                    last_of_unit()

            def att2(st):
                l, tok = st.l, st.tok
                nq = SEQ if st.last else 512
                open_token(tok)
                pe.wait_ge(S.in_act, st.ia)
                cols = qk_cols(st)
                stats(tok, [[SQ2[:, t, P * tt:P * tt + P]] for t, tt in cols], con("two", 2), 2)
                pe.wait_ge(S.rstd, st.rs + 1)
                for b, tiles in enumerate(((0, 4), (4, 8), (8, 12), (12, 13))):
                    tk = tok + 1 + b
                    open_token(tk)
                    for t in range(*tiles):
                        for tt in range((nq if t < 8 else 512) // P):
                            c = 2 * cols.index((t, tt))
                            for h in range(2):
                                mm = pe.matmul(ps(tk)[64 * h:64 * h + 64, t - tiles[0], P * tt:P * tt + P],
                                               RS[:, c + h:c + h + 1].to_broadcast([P, 64]), ident,
                                               start=True, stop=True, skip_group_check=True)
                    mm.then_inc(S.qk_rb, 1)
                tok += 5
                rp = _par[f"rpb{l}"]
                hot = _par["c_hot"]
                for b in range(8):
                    open_token(tok + b)
                    for j in range(8):
                        c2 = 8 * b + j
                        w = CON[0:64, hot + 63 - c2:hot + 191 - c2]
                        mm = pe.matmul(ps(tok + b)[:, 0, 48 * j:48 * j + 48], w, PAR[0:64, rp:rp + 48],
                                       start=True, stop=True, skip_group_check=True)
                    mm.then_inc(S.bias_ps, 1)
                pe.wait_ge(S.roped, l + 1)
                groups(groups2(st))

            table = dict(norm=norm, in1=in1, att1=att1, out=out_proj, up=up, down=down, in2=in2, att2=att2, final=norm)
            pe.wait_ge(S.loaded, 16 * N_LOADS)
            pe.wait_ge(S.at_zero, 1)
            for st in PLAN:
                if st.kind in table:
                    table[st.kind](st)

        @block.scalar
        def _(act):
            def split(ub, m=0):
                v = ub + AHEAD
                if v >= TOTAL["u"]:
                    return
                act.wait_ge(raw_in[v % RING], 16 * (v // RING + 1) + 16 * m)
                wait(act, S.units_done, ub + 4 * m)
                act.activation(W_hi[:, v % RING, :], W_raw[:, v % RING, :], ACT.Copy).then_inc(S.w_hi, 1)

            def done(n):
                act.wait_ge(S.units_done, n)

            def rstd0(rs, n):
                act.wait_ge(S.var, rs + 1)
                act.activation(L_[:, 0:n], V_[:, 0:n], ACT.Ln).then_inc(S.log_var, 1)
                act.wait_ge(S.log_var, rs + 1)
                act.activation(R0[:, 0:n], L_[:, 0:n], ACT.Exp, scale=-0.5).then_inc(S.rstd0, 1)

            def norm(st):
                N = st.N
                h = KT // 2
                after_final = st.blk == 2 and st.l == 0 and st.which == 0
                wait(act, S.evac, st.tok - (0 if after_final else 1))
                act.activation(SQ[:, 0:h, 0:N], X[:, 0:h, 0:N], ACT.Square).then_inc(S.squared_a, 1)
                wait(act, S.evac, st.tok)
                act.activation(SQ[:, h:KT, 0:N], X[:, h:KT, 0:N], ACT.Square).then_inc(S.squared, 1)
                rstd0(st.rs, N // P)
                if st.kind == "final":
                    return
                if st.blk == 2:
                    act.wait_ge(S.gain_ready, 3 * st.l + st.which + 1)
                for kt in range(KT):
                    act.wait_ge(S.scaled, 8 * st.nm + kt + 1)
                    if st.blk == 1:
                        act.activation(H_hi[:, kt, 0:N], TMP[:, kt, 0:N], ACT.Copy).then_inc(S.h_hi, 1)
                    else:
                        for hf in halves(N):
                            c = slice(SEQ * hf, SEQ * hf + SEQ)
                            a = act.activation(H_hi[:, kt, c], TMP[:, kt, c], ACT.Identity,
                                               bias=shift_of(st, kt, hf))
                        a.then_inc(S.h_hi, 1)

            def exps(g):
                act.wait_ge(S.negmax, g.i + 1)
                b = g.i % 2
                for h in range(2):
                    a = act.activation(PR[:, b, h, 0:g.nk], ps(g.tok)[:, h, 0:g.nk], ACT.Exp,
                                       bias=NM[:, b, h:h + 1], scale=g.scale, accum_out=SM[:, b, h:h + 1])
                a.then_inc(S.probs_exp, 1)
                if g.sink is not None:
                    for h in range(2):
                        a = act.activation(ES[:, b, h:h + 1], g.sink(h), ACT.Exp, bias=NM[:, b, h:h + 1])
                    a.then_inc(S.sink_exp, 1)

            def probs_t(g):
                act.wait_ge(S.probsT, g.i + 1)
                act.activation(PTS[:, g.i % 2, :, 0:g.nk], ps(g.tok)[:, 2:4, 0:g.nk], ACT.Copy)\
                   .then_inc(S.probsT_sb, 1)

            def y_part(g):
                if g.out is None:
                    return
                act.wait_ge(S.pv, g.i + 1)
                act.activation(H_hi[g.out], ps(g.tok)[:, 0, 0:P], ACT.Copy).then_inc(S.y_hi, 1)

            def groups(gs, extra=()):
                extra = list(extra)
                exps(gs[0])
                for i, g in enumerate(gs):
                    if i:
                        y_part(gs[i - 1])
                    if extra:
                        extra.pop(0)()
                    probs_t(g)
                    if i + 1 < len(gs):
                        exps(gs[i + 1])
                y_part(gs[-1])

            def in1(st):
                l, tok, u = st.l, st.tok, st.u
                for j in range(st.n_units):
                    split(u + j)
                    if j == 4:
                        done(u + 4)
                        act.activation(SGM[:, :, :], ps(tok)[:, 2:4, 0:SEQ], ACT.Sigmoid).then_inc(S.sig, 1)
                done(u + 23)
                act.activation(SR[:, :, :], ps(tok + 5)[:, :, 0:SEQ], ACT.Silu).then_inc(S.in_act, 1)

            def att1(st):
                l = st.l
                act.wait_ge(S.gate_logits, l + 1)
                for t in range(2):
                    act.activation(Z[:, t, :], ps(st.tok)[:, 0, SEQ * t:SEQ * t + SEQ], ACT.Abs,
                                   bias=par1(f"gate_b{l}", t)).then_inc(S.gate_abs, 1)
                act.wait_ge(S.gate_abs, 2 * (l + 1))
                act.activation(EG[:, :, :], Z[:, :, :], ACT.Exp, scale=-1.0).then_inc(S.gate_e, 1)
                act.wait_ge(S.gate_e, l + 1)
                act.activation(EN[:, :, :], EG[:, :, :], ACT.Ln, bias=1.0).then_inc(S.gate_l, 1)

                def decay():
                    act.wait_ge(S.gate_d, l + 1)
                    act.activation(EG[:, :, :], GS[:, :, :], ACT.Exp, scale=1.0 / 16).then_inc(S.gate_exps, 1)
                    act.activation(EN[:, :, :], GS[:, :, :], ACT.Exp, scale=-1.0 / 16).then_inc(S.gate_exps, 1)
                    act.activation(ED[:, :, :], Z[:, :, :], ACT.Exp, scale=1.0 / 16).then_inc(S.gate_exps, 1)

                groups(groups1(st), [decay])
                act.wait_ge(S.centered, l + 1)
                act.activation(SQA[:, 0:2, :], AC[:, :, :], ACT.Square).then_inc(S.squared, 1)
                rstd0(st.rs, 2)
                act.wait_ge(S.evac, st.tok + 5)
                act.activation(SQA[:, 2:4, :], OM[:, :, :], ACT.Square).then_inc(S.squared, 1)
                rstd0(st.rs + 1, 8)
                act.wait_ge(S.evac, st.tok + 8)
                act.activation(SQA[:, 4:8, :], OG[:, :, :], ACT.Square).then_inc(S.squared, 1)
                rstd0(st.rs + 2, 8)
                act.wait_ge(S.ln_out, l + 1)
                for t in range(2):
                    a = act.activation(Y[:, t, :], TMPA[:, t, :], ACT.Silu, bias=par1(f"ln_b{l}", t))
                a.then_inc(S.ln_act, 1)
                act.wait_ge(S.ln_act, l + 1)
                act.activation(H_hi[:, 0:2, 0:SEQ], Y[:, 0:2, :], ACT.Copy).then_inc(S.mix_hi, 1)
                act.wait_ge(S.mix_y, 2 * l + 1)
                act.activation(H_hi[:, 2:4, 0:SEQ], Y[:, 2:4, :], ACT.Copy).then_inc(S.mix_hi, 1)
                act.wait_ge(S.mix_y, 2 * l + 2)
                act.activation(H_hi[:, 4:8, 0:SEQ], Y[:, 4:8, :], ACT.Copy).then_inc(S.mix_hi, 1)

            def plain(st):
                for j in range(st.n_units):
                    split(st.u + j)

            def up(st):
                N = st.N
                if st.blk == 1:
                    def post(j, t, m):
                        if j == 0:
                            act.wait_ge(S.units_done, st.u + 4 + 4 * m)
                            o = _par[f"ffn_conv{st.l}"]
                            for b in range(4):
                                c = o + 4 * b + 16 * m
                                act.activation(U[:, b, :], ps(t)[:, b, 0:SEQ], ACT.Identity,
                                               scale=PAR[:, bass.ds(c + 2, 1)], bias=PAR[:, bass.ds(c + 3, 1)])\
                                   .then_inc(S.biased, 1)
                        if j == 1:
                            act.wait_ge(S.evac, st.tok + 1 + m)
                            act.activation(SG[:, 0:2 * SEQ], U[:, 0:2, :].rearrange("p a b -> p (a b)"), ACT.Silu)\
                               .then_inc(S.silued, 1)
                        if j == 2:
                            act.wait_ge(S.hid_f32, st.hid + m + 1)
                            act.activation(HID_hi[:, bass.ds(512 * m, 512)], HF[:, 0:512], ACT.Copy)\
                               .then_inc(S.hid_hi, 1)
                else:
                    def post(j, t, m):
                        if j == 0:
                            act.wait_ge(S.units_done, st.u + 4 + 4 * m)
                            act.activation(SG[:, 0:2 * N].rearrange("p (a b) -> p a b", a=2), ps(t)[:, 0:2, 0:N],
                                           ACT.Silu).then_inc(S.silued, 1)
                        if j == 2:
                            act.wait_ge(S.evac, st.tok + 1 + m)
                            act.activation(HID_hi[:, bass.ds(2 * N * m, 2 * N)], HF[:, 0:2 * N], ACT.Copy)\
                               .then_inc(S.hid_hi, 1)
                up_loop(act, st, split, post)

            def in2(st):
                u, tok = st.u, st.tok
                nq = SEQ if st.last else 512
                ends = {4: (0, 4, nq), 8: (4, 8, nq), 12: (8, 12, 512)}

                def square(j):
                    a, b, n = ends[j]
                    done(u + j)
                    act.activation(SQ2[:, a:b, 0:n], ps(tok + j // 4 - 1)[:, :, 0:n], ACT.Square)\
                       .then_inc(S.in_act, 1)

                for j in range(st.n_units):
                    split(u + j)
                    if j in ends:
                        square(j)
                done(u + 18)
                act.activation(SQ2[:, 12, :], ps(tok + 4)[:, 0, :], ACT.Square).then_inc(S.in_act, 1)

            def att2(st):
                rstd0(st.rs, 2 * len(qk_cols(st)))
                groups(groups2(st))

            table = dict(norm=norm, final=norm, in1=in1, att1=att1, out=plain, down=plain, up=up, in2=in2, att2=att2)
            act.wait_ge(S.loaded, 16 * N_LOADS)
            act.activation(SC[:, :, :], SC[:, :, :], ACT.Silu)\
               .then_inc(S.cond_ready, 1)
            for v in range(AHEAD):
                split(v - AHEAD)
            for st in PLAN:
                if st.kind in table:
                    table[st.kind](st)

        @block.vector
        def _(dve):
            count = Counter()

            def split(ub, m=0):
                v = ub + AHEAD
                if v >= TOTAL["u"]:
                    return
                dve.wait_ge(S.w_hi, v + 1 + 4 * m)
                dve.tensor_tensor(W_lo[:, v % RING, :], W_raw[:, v % RING, :], W_hi[:, v % RING, :].bitcast(F32),
                                  ALU.subtract).then_inc(S.w_lo, 1)

            def step(ins):
                count.steps += 1
                ins.then_inc(S.dve_step, 1)
                dve.wait_ge(S.dve_step, count.steps)

            def rstd(rs, src, n, size, eps):
                dve.wait_ge(S.stats, rs + 1)
                dve.tensor_scalar(V_[:, 0:n], src, 1.0 / size, eps, ALU.mult, ALU.add).then_inc(S.var, 1)
                dve.wait_ge(S.rstd0, rs + 1)
                step(dve.scalar_tensor_tensor(T_[:, 0:n], R0[:, 0:n], -0.5, R0[:, 0:n], ALU.mult, ALU.mult))
                step(dve.tensor_tensor(T_[:, 0:n], T_[:, 0:n], V_[:, 0:n], ALU.mult))
                dve.scalar_tensor_tensor(RS[:, 0:n], T_[:, 0:n], 1.5, R0[:, 0:n], ALU.add, ALU.mult)\
                   .then_inc(S.rstd, 1)

            def release(sem, value):
                dve.wait_ge(sem, value)
                dve.sem_inc(S.evac, 1)

            def norm(st):
                N, tok = st.N, st.tok
                if st.blk == 2:
                    dve.wait_ge(S.gain_ready, 3 * st.l + st.which + 1)
                rstd(st.rs, ps(tok)[:, 0, 0:N // P], N // P, D, EPS)
                dve.wait_ge(S.rstd_b, st.sq + 1)
                wait(dve, S.evac, st.tok)
                if st.kind == "final":
                    for kt in range(KT):
                        a = dve.scalar_tensor_tensor(X[:, kt, 0:N], X[:, kt, 0:N], par1("final_g", kt),
                                                     ps(tok)[:, 1, 0:N], ALU.mult, ALU.mult)
                    a.then_inc(S.evac, 1)
                    return
                def scale(kt):
                    for hf in halves(N):
                        c = slice(SEQ * hf, SEQ * hf + SEQ)
                        a = dve.scalar_tensor_tensor(TMP[:, kt, c], X[:, kt, c], gain_of(st, kt, hf),
                                                     ps(tok)[:, 1, c], ALU.mult, ALU.mult)
                    a.then_inc(S.scaled, 1)

                def low(kt):
                    dve.wait_ge(S.h_hi, 8 * st.nm + kt + 1)
                    for hf in halves(N):
                        c = slice(SEQ * hf, SEQ * hf + SEQ)
                        if st.blk == 1:
                            a = dve.tensor_tensor(H_lo[:, kt, c], TMP[:, kt, c], H_hi[:, kt, c].bitcast(F32),
                                                  ALU.subtract)
                        else:
                            a = dve.scalar_tensor_tensor(H_lo[:, kt, c], TMP[:, kt, c], shift_of(st, kt, hf),
                                                         H_hi[:, kt, c].bitcast(F32), ALU.add, ALU.subtract)
                    a.then_inc(S.h_ready, 1)

                for kt in range(KT):
                    scale(kt)
                    if kt:
                        low(kt - 1)
                release(S.scaled, 8 * st.nm + 8)
                low(KT - 1)

            def done(n):
                dve.wait_ge(S.units_done, n)

            def maxima(g):
                dve.wait_ge(S.scores, g.i + 1)
                b = g.i % 2
                sc = ps(g.tok)[:, 0:2, 0:g.nk]
                if g.mask is not None:
                    w = g.mask.shape[2]
                    step(dve.tensor_tensor(ps(g.tok)[:, 0:2, 0:w], ps(g.tok)[:, 0:2, 0:w], g.mask, ALU.add))
                if g.sink is None and g.scale == 1.0:
                    dve.tensor_reduce(NM[:, b, :], sc, AX.X, ALU.max, negate=True).then_inc(S.negmax, 1)
                else:
                    step(dve.tensor_reduce(NM[:, b, :], sc, AX.X, ALU.max, negate=True))
                    if g.sink is None:
                        dve.tensor_scalar(NM[:, b, :], NM[:, b, :], g.scale, None, ALU.mult).then_inc(S.negmax, 1)
                    else:
                        step(dve.tensor_scalar(ES[:, b, :], g.sinks, -1.0, None, ALU.mult))
                        dve.tensor_tensor(NM[:, b, :], NM[:, b, :], ES[:, b, :], ALU.min).then_inc(S.negmax, 1)

            def normalise(g):
                dve.wait_ge(S.probs_exp, g.i + 1)
                b = g.i % 2
                if g.sink is not None:
                    dve.wait_ge(S.sink_exp, g.si + 1)
                    step(dve.tensor_tensor(SM[:, b, :], SM[:, b, :], ES[:, b, :], ALU.add))
                step(dve.reciprocal(RI[:, b, :], SM[:, b, :]))
                for h in range(2):
                    a = dve.tensor_scalar(PR[:, b, h, 0:g.nk], PR[:, b, h, 0:g.nk], RI[:, b, h:h + 1], None, ALU.mult)
                a.then_inc(S.probs, 1)

            def result(g):
                if g.out is None:
                    dve.wait_ge(S.pv, g.i + 1)
                    dve.tensor_copy(g.dst, ps(g.tok)[:, 0, 0:P]).then_inc(S.evac, 1)
                else:
                    dve.wait_ge(S.y_hi, g.yi + 1)
                    dve.tensor_tensor(H_lo[g.out], ps(g.tok)[:, 0, 0:P], H_hi[g.out].bitcast(F32), ALU.subtract)\
                       .then_inc(S.evac, 1)

            def groups(gs, extra=()):
                extra = list(extra)
                maxima(gs[0])
                if extra:
                    extra.pop(0)()
                for i, g in enumerate(gs):
                    normalise(g)
                    if i:
                        result(gs[i - 1])
                    if i + 1 < len(gs):
                        maxima(gs[i + 1])
                    if extra:
                        extra.pop(0)()
                result(gs[-1])

            def in1(st):
                l, tok, u = st.l, st.tok, st.u
                taps = [(k, t) for k in range(TAPS) for t in range(2)]
                t0 = 2 * TAPS * l

                def tap():
                    if not taps:
                        return
                    k, t = taps.pop(0)
                    n = 2 * k + t
                    w = par1(f"conv_w{l}", 2 * k + t)
                    src = HC[:, t, k:k + SEQ]
                    if k == 0:
                        dve.tensor_scalar(AC[:, t, :], src, w, par1(f"conv_b{l}", t), ALU.mult, ALU.add)\
                           .then_inc(S.tap, 1)
                    else:
                        dve.wait_ge(S.tap, t0 + n - 1)
                        dve.scalar_tensor_tensor(AC[:, t, :], src, w, AC[:, t, :], ALU.mult, ALU.add)\
                           .then_inc(S.tap, 1)

                for j in range(st.n_units + 1):
                    if j < st.n_units:
                        split(u + j)
                    if j == 4:
                        done(u + 4)
                        dve.memset(HC[:, :, 0:HALO], 0.0)
                        dve.wait_ge(S.sig, l + 1)
                        dve.tensor_tensor(HC[:, :, HALO:HALO + SEQ], ps(tok)[:, 0:2, 0:SEQ], SGM[:, :, :], ALU.mult)\
                           .then_inc(S.evac, 1)
                        dve.wait_ge(S.evac, tok + 1)
                    if j == 8:
                        done(u + 8)
                        dve.tensor_copy(Q[:, 0:2, 0:SEQ], ps(tok + 1)[:, 0:2, 0:SEQ])
                        dve.tensor_copy(KM[:, 0:2, 0:SEQ], ps(tok + 1)[:, 2:4, 0:SEQ]).then_inc(S.evac, 1)
                    if j == 11:
                        done(u + 11)
                        dve.tensor_copy(V[:, 0:2, 0:SEQ], ps(tok + 2)[:, 0:2, 0:SEQ])
                        dve.tensor_copy(GG[0:16, :], ps(tok + 2)[0:16, 2, 0:SEQ]).then_inc(S.evac, 1)
                    if j == 15:
                        done(u + 15)
                        dve.tensor_copy(QG[:, :, :], ps(tok + 3)[:, 0:2, 0:SEQ])
                        dve.tensor_copy(KG[:, :, :], ps(tok + 3)[:, 2:4, 0:SEQ]).then_inc(S.evac, 1)
                    if j == 19:
                        done(u + 19)
                        dve.tensor_copy(VG[:, :, :], ps(tok + 4)[:, 0:2, :]).then_inc(S.evac, 1)
                    if j > 4:
                        for _ in range(4):
                            tap()
                while taps:
                    tap()
                release(S.in_act, st.ia + 1)

            def att1(st):
                l, tok = st.l, st.tok
                dve.wait_ge(S.evac, tok)
                dve.wait_ge(S.gate_abs, 2 * (l + 1))
                lg = ps(tok)[:, 0, :].rearrange("p (t n) -> p t n", t=2)
                for t in range(2):
                    b = par1(f"gate_b{l}", t)
                    dve.tensor_scalar(LA[:, t, :], lg[:, t, :], b, 0.0, ALU.add, ALU.min).then_inc(S.gate_min, 1)
                release(S.gate_min, 2 * (l + 1))

                def cumulate():
                    dve.wait_ge(S.gate_l, l + 1)
                    step(dve.tensor_tensor(LA[:, :, :], LA[:, :, :], EN[:, :, :], ALU.subtract))
                    for t in range(2):
                        a = dve.tensor_tensor_scan(GS[:, t, :], con("reset", 256), LA[:, t, :], 0.0, ALU.mult, ALU.add)
                    step(a)
                    g4 = GS[:, :, :].rearrange("p t (c n) -> p (t c) n", n=CHUNK)
                    z4 = Z[:, :, :].rearrange("p t (c n) -> p (t c) n", n=CHUNK)
                    dve.tensor_tensor(z4, g4[:, :, CHUNK - 1:CHUNK].to_broadcast([P, 2 * NCH, CHUNK]), g4,
                                      ALU.subtract).then_inc(S.gate_d, 1)

                def decay():
                    dve.wait_ge(S.gate_exps, 3 * (l + 1))
                    dve.tensor_tensor(KD[:, :, :], KG[:, :, :], ED[:, :, :], ALU.mult)
                    dve.scalar_tensor_tensor(flat(QG[:, :, :]), flat(QG[:, :, :]), 0.125, flat(EG[:, :, :]), ALU.mult,
                                             ALU.mult)
                    dve.tensor_tensor(KG[:, :, :], KG[:, :, :], EN[:, :, :], ALU.mult).then_inc(S.gla_in, 1)

                groups(groups1(st), [cumulate, decay])
                tok += 5
                dve.wait_ge(S.kdT, l + 1)
                dve.tensor_copy(KDT[:, :, :], ps(tok)[:, 0, :].rearrange("p (t n) -> p t n", t=2))\
                   .then_inc(S.kdT_sb, 1)
                dve.wait_ge(S.attnT, l + 1)
                dve.wait_ge(S.at_zero, 1)
                for par_ in range(2):
                    a = dve.copy_predicated(AT[:, 4 * par_:4 * par_ + 4, :], bcast_mid(MASKI[:, :], 4),
                                            ps(tok)[:, 1 + par_, :].rearrange("p (t n) -> p t n", t=4))
                a.then_inc(S.attn_sb, 1)
                release(S.attn_sb, l + 1)
                tok += 1
                dve.wait_ge(S.d_state, l + 1)
                for pair in range(2):
                    dve.memset(ST[:, 0, pair, :], 0.0).then_inc(S.state, 1)
                for c in range(NCH - 1):
                    for pair in range(2):
                        ds = ps(tok)[:, c % 4, (c // 4) * 256 + pair * 128:(c // 4) * 256 + pair * 128 + P]
                        dve.wait_ge(S.state, 16 * l + 2 * c + pair + 1)
                        e = CHUNK * c + CHUNK - 1
                        dve.scalar_tensor_tensor(ST[:, c + 1, pair, :], ST[:, c, pair, :], EG[:, pair, e:e + 1], ds,
                                                 ALU.mult, ALU.add).then_inc(S.state, 1)
                release(S.state, 16 * (l + 1))
                tok += 1
                dve.wait_ge(S.gla_o, l + 1)
                dve.tensor_copy(OG[:, 0:2, :], ps(tok)[:, 0, :].rearrange("p (t n) -> p t n", t=2))
                dve.tensor_copy(OG[:, 2:4, :], ps(tok)[:, 1, :].rearrange("p (t n) -> p t n", t=2))\
                   .then_inc(S.evac, 1)
                tok += 1
                dve.wait_ge(S.mu, l + 1)
                dve.tensor_tensor(AC[:, :, :], AC[:, :, :], bcast_mid(ps(tok)[:, 2, 0:SEQ], 2), ALU.subtract)\
                   .then_inc(S.centered, 1)
                rstd(st.rs, ps(tok)[:, 0, 0:2], 2, 2 * P, LN_EPS)
                dve.wait_ge(S.rstd_b, st.sq + 1)
                for t in range(2):
                    a = dve.scalar_tensor_tensor(TMPA[:, t, :], AC[:, t, :], par1(f"ln_g{l}", t),
                                                 ps(tok)[:, 1, 0:SEQ], ALU.mult, ALU.mult)
                a.then_inc(S.ln_out, 1)
                release(S.ln_out, l + 1)
                tok += 1
                rstd(st.rs + 1, ps(tok)[:, 0, 0:8], 8, 64, EPS)
                dve.wait_ge(S.rstd_b, st.sq + 2)
                for t in range(2):
                    a = dve.scalar_tensor_tensor(Y[:, 2 + t, :], OM[:, t, :], par1(f"moba_g{l}", t),
                                                 ps(tok)[:, 1, SEQ * t:SEQ * t + SEQ], ALU.mult, ALU.mult)
                a.then_inc(S.mix_y, 1)
                release(S.mix_y, 2 * l + 1)
                tok += 1
                rstd(st.rs + 2, ps(tok)[:, 0, 0:8], 8, P, EPS)
                dve.wait_ge(S.rstd_b, st.sq + 3)
                for i, h in enumerate((0, 2, 1, 3)):
                    a = dve.scalar_tensor_tensor(OG[:, i, :], OG[:, i, :], par1(f"gla_g{l}", h),
                                                 ps(tok)[:, 1 + i // 2, SEQ * (i % 2):SEQ * (i % 2) + SEQ],
                                                 ALU.mult, ALU.mult)
                a.then_inc(S.evac, 1)
                dve.wait_ge(S.evac, tok + 1)
                for i, h in enumerate((0, 2, 1, 3)):
                    a = dve.tensor_tensor(Y[:, 4 + h, :], OG[:, i, :], SR[:, h, :], ALU.mult)
                a.then_inc(S.mix_y, 1)
                for i, (a_, b_, n) in enumerate(((0, 2, 2), (2, 4, 2), (4, 8, 4))):
                    dve.wait_ge(S.mix_hi, 3 * l + i + 1)
                    for kt in range(a_, b_):
                        dve.tensor_tensor(H_lo[:, kt, 0:SEQ], Y[:, kt, :], H_hi[:, kt, 0:SEQ].bitcast(F32),
                                          ALU.subtract).then_inc(S.h_ready, 1)

            def update(st, tok, m, end):
                done(end)
                dve.wait_ge(S.evac, tok)
                if st.blk == 1:
                    dve.tensor_tensor(X[:, 4 * m:4 * m + 4, 0:SEQ], ps(tok)[:, :, 0:SEQ],
                                      X[:, 4 * m:4 * m + 4, 0:SEQ], ALU.add).then_inc(S.evac, 1)
                else:
                    for t in range(4):
                        for hf in halves(st.N):
                            c = slice(SEQ * hf, SEQ * hf + SEQ)
                            a = dve.scalar_tensor_tensor(X[:, 4 * m + t, c], ps(tok)[:, t, c],
                                                         GATE[:, st.gate, 4 * m + t, hf:hf + 1],
                                                         X[:, 4 * m + t, c], ALU.mult, ALU.add)
                    a.then_inc(S.evac, 1)

            def out_proj(st):
                for j in range(8):
                    split(st.u + j)
                    if j == 4:
                        update(st, st.tok, 0, st.u + 4)
                update(st, st.tok + 1, 1, st.u + 8)

            def down(st):
                n = st.pairs
                for j in range(2 * n):
                    split(st.u + j)
                    if j == n:
                        update(st, st.tok, 0, st.u + n)
                update(st, st.tok + 1, 1, st.u + 2 * n)

            def up(st):
                N = st.N
                if st.blk == 1:
                    def post(j, t, m):
                        if j == 0:
                            o = _par[f"ffn_conv{st.l}"]
                            for k in (1, 2):
                                for b in range(4):
                                    if k == 1:
                                        dve.wait_ge(S.biased, 4 * (st.hid) + 4 * m + b + 1)
                                    else:
                                        dve.wait_ge(S.conv1, 4 * (st.hid) + 4 * m + b + 1)
                                    c = o + 4 * b + 16 * m + 2 - k
                                    a = dve.scalar_tensor_tensor(U[:, b, k:SEQ], ps(t)[:, b, 0:SEQ - k],
                                                                 PAR[:, bass.ds(c, 1)], U[:, b, k:SEQ], ALU.mult, ALU.add)
                                    if k == 1:
                                        a.then_inc(S.conv1, 1)
                            a.then_inc(S.evac, 1)
                        if j == 2:
                            dve.wait_ge(S.silued, st.hid + m + 1)
                            dve.tensor_tensor(HF[:, 0:512], SG[:, 0:512], U[:, 2:4, :].rearrange("p a b -> p (a b)"),
                                              ALU.mult).then_inc(S.hid_f32, 1)
                        if j == 3:
                            dve.wait_ge(S.hid_hi, st.hid + m + 1)
                            c = bass.ds(512 * m, 512)
                            dve.tensor_tensor(HID_lo[:, c], HF[:, 0:512], HID_hi.bitcast(F32)[:, c], ALU.subtract)\
                               .then_inc(S.hid_ready, 1)
                else:
                    def post(j, t, m):
                        if j == 1:
                            dve.wait_ge(S.silued, st.hid + m + 1)
                            wait(dve, S.hid_ready, st.hid + m)
                            dve.tensor_tensor(HF[:, 0:2 * N].rearrange("p (a b) -> p a b", a=2),
                                              SG[:, 0:2 * N].rearrange("p (a b) -> p a b", a=2),
                                              ps(t)[:, 2:4, 0:N], ALU.mult).then_inc(S.evac, 1)
                        if j == 3:
                            dve.wait_ge(S.hid_hi, st.hid + m + 1)
                            c = bass.ds(2 * N * m, 2 * N)
                            dve.tensor_tensor(HID_lo[:, c], HF[:, 0:2 * N], HID_hi.bitcast(F32)[:, c], ALU.subtract)\
                               .then_inc(S.hid_ready, 1)
                up_loop(dve, st, split, post)

            def mods(st):
                l, w = st.l, st.which
                a = 3 * KT * w
                dve.wait_ge(S.mod_sums, MODS * l + a + 3 * KT)
                o = _par[f"b_ada{l}"] + a
                m = MOD[:, l, a:a + 3 * KT, :]
                step(dve.tensor_tensor(m, m, bcast_last(PAR[:, o:o + 3 * KT], 2), ALU.add))
                o = _par[f"norm_g{l}"] + KT * w
                step(dve.tensor_scalar(GAIN[:, w, :, :], m[:, KT:2 * KT, :], 1.0, None, ALU.add))
                dve.tensor_tensor(GAIN[:, w, :, :], GAIN[:, w, :, :], bcast_last(PAR[:, o:o + KT], 2), ALU.mult)
                dve.tensor_scalar(GATE[:, w, :, :], m[:, 2 * KT:, :], 1.0 if w == 1 else 0.5, None, ALU.mult)\
                    .then_inc(S.gain_ready, 1)

            def in2(st):
                u, tok = st.u, st.tok
                nq = SEQ if st.last else 512
                for j in range(st.n_units + 1):
                    if j < st.n_units:
                        split(u + j)
                    if j in (4, 8, 12):
                        dve.wait_ge(S.in_act, st.ia + j // 4)
                        m = j // 4 - 1
                        dst = (Q[:, 0:4, 0:nq], Q[:, 4:8, 0:nq], KM[:, 0:4, :])[m]
                        dve.tensor_copy(dst, ps(tok + m)[:, :, 0:(nq if m < 2 else 512)]).then_inc(S.evac, 1)
                    if j == 16:
                        done(u + 16)
                        dve.tensor_copy(V[:, :, 0:512], ps(tok + 3)[:, :, :]).then_inc(S.evac, 1)
                    if j == 18:
                        dve.wait_ge(S.in_act, st.ia + 4)
                        dve.tensor_copy(KM[:, 4, :], ps(tok + 4)[:, 0, :])
                        dve.tensor_copy(V[:, :, 512:640], ps(tok + 4)[:, 1, :].rearrange("p (t n) -> p t n", t=4))\
                           .then_inc(S.evac, 1)

            def att2(st):
                l, tok = st.l, st.tok
                nq = SEQ if st.last else 512
                n = 2 * len(qk_cols(st))
                dve.wait_ge(S.evac, tok)
                rstd(st.rs, ps(tok)[:, 0, 0:n], n, 64, EPS)
                release(S.rstd, st.rs + 1)
                for b, (dst, gi, scale, w) in enumerate(((Q[:, 0:4, 0:nq], 0, 0.125, nq), (Q[:, 4:8, 0:nq], 2, 0.125, nq),
                                                         (KM[:, 0:4, :], 1, 1.0, 512), (KM[:, 4:5, :], 3, 1.0, 512))):
                    dve.wait_ge(S.qk_rb, 4 * l + b + 1)
                    k = dst.shape[1]
                    if scale != 1.0:
                        step(dve.tensor_scalar(T_[:, 1:2], par1(f"qk_g{l}", gi), scale, None, ALU.mult))
                        gcol = T_[:, 1:2]
                    else:
                        gcol = par1(f"qk_g{l}", gi)
                    dve.scalar_tensor_tensor(dst, dst, gcol, ps(tok + 1 + b)[:, 0:k, 0:w], ALU.mult, ALU.mult)\
                       .then_inc(S.evac, 1)
                    dve.wait_ge(S.evac, tok + 2 + b)
                swap = [(i + 16) % 32 for i in range(32)]
                dve.stream_shuffle(ROT[:, 0:4, :], Q[:, 4:8, 0:SEQ], swap)
                step(dve.stream_shuffle(ROT[:, 4, :], KM[:, 4, 0:SEQ], swap))
                cos, sin = con("cos", 256), con("sin", 256)
                dve.tensor_tensor(Q[:, 4:8, 0:SEQ], Q[:, 4:8, 0:SEQ], bcast_mid(cos, 4), ALU.mult)
                dve.tensor_tensor(KM[:, 4, 0:SEQ], KM[:, 4, 0:SEQ], cos, ALU.mult)
                step(dve.tensor_tensor(ROT[:, :, :], ROT[:, :, :], bcast_mid(sin, 5), ALU.mult))
                dve.tensor_tensor(Q[:, 4:8, 0:SEQ], Q[:, 4:8, 0:SEQ], ROT[:, 0:4, :], ALU.add)
                dve.tensor_tensor(KM[:, 4, 0:SEQ], KM[:, 4, 0:SEQ], ROT[:, 4, :], ALU.add).then_inc(S.roped, 1)
                tok += 5
                o = _par["c_colmask"]
                for b in range(8):
                    dve.wait_ge(S.bias_ps, 8 * l + b + 1)
                    src = ps(tok + b)[:, 0, 0:384].rearrange("p (c n) -> p n c", n=48)
                    dve.tensor_tensor(BT[:, :, 8 * b:8 * b + 8], src, bcast_mid(CON[:, o + 8 * b:o + 8 * b + 8], 48),
                                      ALU.add).then_inc(S.evac, 1)
                dve.wait_ge(S.evac, tok + 8)
                groups(groups2(st))

            table = dict(norm=norm, final=norm, in1=in1, att1=att1, out=out_proj, down=down, up=up,
                         mods=mods, in2=in2, att2=att2)
            dve.wait_ge(S.loaded, 16 * N_LOADS)
            for v in range(AHEAD):
                split(v - AHEAD)
            for st in PLAN:
                if st.kind in table:
                    table[st.kind](st)


def _constants():
    C_ = np.zeros((P, N_CONST), np.float32)

    def put(name, a):
        o = _par["c_" + name]
        a = a.reshape(a.shape[0], -1)
        C_[:a.shape[0], o:o + a.shape[1]] = a

    p = np.arange(P)
    put("ident", np.eye(P))
    put("ones", np.ones((P, 2)))
    put("mean256", np.full((P, P), 1.0 / 256))
    put("two", np.stack([p < 64, p >= 64], 1))
    k = np.arange(SEQ)
    q = p[:, None, None] + P * np.arange(2)[None, :, None]
    put("causal", np.where(k[None, None] <= q, 0.0, BIG))
    put("band", np.where(k[None] >= p[:, None], 0.0, BIG))
    c = p[:, None] % 64
    c2 = np.arange(64)[None]
    c0 = np.clip(c - 8, 0, 48)
    put("colmask", np.where((c2 >= c0) & (c2 < c0 + 16), 0.0, BIG))
    put("reset", np.tile(k[None] % CHUNK != 0, (P, 1)))
    inv = (np.float32(10000.0) ** (-np.arange(0, 32, 2, dtype=np.float32) / np.float32(32))).astype(np.float32)
    pos = np.stack([k // 64, k % 64]).astype(np.float32)
    ang = pos[(p % 64) // 32] * inv[p % 16][:, None]
    put("cos", np.cos(ang, dtype=np.float32))
    put("sin", np.where(p[:, None] % 32 < 16, -1, 1) * np.sin(ang, dtype=np.float32))
    hot = np.zeros((64, 191))
    for half in range(2):
        for dc in range(31):
            hot[32 * half + dc, 78 - dc + 64 * half] = 1
    put("hot", hot)
    i, j = np.arange(P)[None], np.arange(P)[:, None]
    return C_, ((i // CHUNK == j // CHUNK) & (j <= i)).astype(np.int32)


def _columns(v):
    return v.reshape(-1, P).T


def _parameters(a):
    out = np.zeros((P, N_PAR), np.float32)

    def put(name, v):
        o = _par[name]
        out[:v.shape[0], o:o + v.shape[1]] = v

    for l in range(DEPTH):
        put(f"mix_g{l}", _columns(a["norm_mix_g"][l]))
        put(f"ffn_g{l}", _columns(a["norm_ffn_g"][l]))
        put(f"conv_w{l}", a["conv_w"][l].reshape(TAPS, 2, P).transpose(2, 0, 1).reshape(P, -1))
        for n, src in (("conv_b", "conv_b"), ("ln_g", "conv_ln_g"), ("ln_b", "conv_ln_b"), ("moba_g", "moba_out_g"),
                       ("gate_b", "gla_gate_b"), ("gla_g", "gla_out_g")):
            put(f"{n}{l}", _columns(a[src][l]))
        w = np.concatenate([a["ffn_conv_w"][l], a["ffn_conv_b"][l][None]])
        w = w.reshape(4, 2, PAIRS, 2, P).transpose(4, 2, 1, 3, 0)
        put(f"ffn_conv{l}", w.reshape(P, -1))
        put(f"norm_g{l}", _columns(a["norm_g_2"][l].reshape(-1)))
        put(f"b_ada{l}", _columns(a["b_ada_2"][l]))
        put(f"qk_g{l}", np.concatenate([a["qk_norm_g_2"][l].T] * 2))
        put(f"sink{l}", np.broadcast_to(a["wa_sink_2"][l][[0, 4, 1, 5, 2, 6, 3, 7]], (P, 8)))
        put(f"gate_w{l}", a["gla_gate_w"][l])
        r = a["na_rpb_2"][l].transpose(2, 0, 1)
        o = _par[f"rpb{l}"]
        for half in range(2):
            out[32 * half:32 * half + 31, o:o + 48] = r[:, :, 5 - half:11 - half].reshape(31, 48)
    put("final_g", _columns(a["final_g"]))
    return out


def _stream(a):
    out = np.empty((TOTAL["u"], P, UNIT), np.float32)
    at = [0]

    def unit(block):
        n = block.shape[0] // P
        out[at[0]].reshape(P, n, UNIT // n)[:] = block.reshape(n, P, UNIT // n).transpose(1, 0, 2)
        at[0] += 1

    def columns(w):
        for c in range(0, w.shape[1], 256):
            for kh in range(2):
                unit(w[512 * kh:512 * kh + 512, c:c + 256])

    for st in PLAN:
        assert at[0] == st.u, (st, at)
        if st.kind == "in1":
            w = a["w_in"][st.l]
            columns(w[:, 0:1280])
            unit(w[:, G_COL:G_COL + P])
            columns(w[:, 1280:G_COL])
            columns(w[:, G_COL + 16:MIX_COLS])
        if st.kind == "in2":
            w = a["w_in_2"][st.l]
            columns(w[:, 0:512])
            columns(w[:, 512:1024][:, QB_ORDER])
            columns(w[:, 1024:2304])
        if st.kind == "out":
            w = a["w_out" if st.blk == 1 else "w_out_2"][st.l]
            if st.blk == 2:
                w = np.concatenate([w[0:512], w[512:1024][QB_ORDER]])
            columns(w)
        if st.kind == "up":
            w = a["ffn_w_up"][st.l] if st.blk == 1 else a["w_ffn_up_2"][st.l, st.ffn]
            for m in range(st.m0, st.m0 + st.pairs):
                columns(w[:, 256 * m:256 * m + 256])
                columns(w[:, FF + 256 * m:FF + 256 * m + 256])
        if st.kind == "down":
            w = a["ffn_w_down"][st.l] if st.blk == 1 else a["w_ffn_down_2"][st.l, st.ffn]
            for hf in range(2):
                for j in range(st.m0, st.m0 + st.pairs):
                    unit(w[256 * j:256 * j + 256, 512 * hf:512 * hf + 512])
    return out.reshape(-1, UNIT)


def kernel(**inputs):
    import concourse.bacc as _bacc
    from concourse import mybir as _mybir
    from concourse.bass_utils import run_bass_kernel_spmd as _run

    a = {n: np.asarray(v) for n, v in inputs.items()}
    const, imask = _constants()
    w_ada = a["w_ada_2"].reshape(DEPTH, D, MODS, P).transpose(0, 2, 3, 1)
    arrays = {
        "xT": a["x"][0].T.reshape(KT, P, SEQ).transpose(1, 0, 2),
        "ctxT": a["ctx_2"][0].T.reshape(KT, P, CTX).transpose(1, 0, 2),
        "wstream": _stream(a),
        "adastream": w_ada.reshape(-1, UNIT),
        "par": _parameters(a),
        "const": const,
        "imask": imask,
        "cond": np.broadcast_to(np.stack([a["c_2"][0], a["c_ctx_2"]]), (P, 2, D)),
    }
    arrays = {n: np.ascontiguousarray(v) for n, v in arrays.items()}
    nc = _bacc.Bacc("TRN2", target_bir_lowering=False, num_devices=1)
    args = [nc.dram_tensor(n, v.shape, _mybir.dt.from_np(v.dtype), kind="ExternalInput").ap()
            for n, v in arrays.items()]
    args.append(nc.dram_tensor("outT", (P, KT, SEQ), F32, kind="ExternalOutput").ap())
    build_kernel(nc, *args)
    r = _run(nc, [arrays], core_ids=[0])
    got = r.results[0]["outT"]
    return np.ascontiguousarray(got.transpose(2, 1, 0).reshape(1, SEQ, D))
```
